# Optimizing a Trainium2 kernel written in Bass

```python
import jax, jax.numpy as jnp
from jax import lax
import numpy as np

D_MODEL = 1024
BATCH = 1
SEQ = 512
DEPTH = 2

N_META = 16
MIX_WIDTH = D_MODEL
POOL_WIDTH = MIX_WIDTH // 2
POOL_GROUPS = 4
POOL_GROUP_DIM = POOL_WIDTH // POOL_GROUPS
POOL_WINDOWS = (2, 4, 8, 16)
GLA_WIDTH = MIX_WIDTH - POOL_WIDTH
GLA_HEADS = 4
GLA_KEY_WIDTH = GLA_WIDTH // 2
GLA_DK = GLA_KEY_WIDTH // GLA_HEADS
GLA_DV = GLA_WIDTH // GLA_HEADS
GLA_GATE_RANK = 16
GLA_GATE_TEMP = 16.0
GLA_CHUNK = 64
GLA_PAD = GLA_CHUNK - N_META
D_FF = 2816
IN_PROJ_COLS = POOL_WIDTH + 2 * GLA_KEY_WIDTH + 2 * GLA_WIDTH + GLA_GATE_RANK
DEEPNORM_ALPHA = (2.0 * DEPTH) ** 0.25
DEEPNORM_BETA = (8.0 * DEPTH) ** -0.25
LN_EPS = 1e-5
RMS_EPS = 1e-6

kernel_name = "hymba_pool_gla_macaron_deepnorm"

def layer_norm(x, g, b):
    xf = x.astype(jnp.float32)
    mu = jnp.mean(xf, axis=-1, keepdims=True)
    var = jnp.mean(jnp.square(xf - mu), axis=-1, keepdims=True)
    y = (xf - mu) * lax.rsqrt(var + LN_EPS)
    return (y * g.astype(jnp.float32) + b.astype(jnp.float32)).astype(x.dtype)

def swiglu(x, w_gate, w_up, w_down):
    return (jax.nn.silu(x @ w_gate) * (x @ w_up)) @ w_down

def pool_mixer(u, w_pool, pool_scale):
    B_, T, _ = u.shape
    uf = u.astype(jnp.float32)
    cs = jnp.cumsum(uf, axis=1)
    t = jnp.arange(T)
    outs = []
    for gi, w in enumerate(POOL_WINDOWS):
        sl = slice(gi * POOL_GROUP_DIM, (gi + 1) * POOL_GROUP_DIM)
        c = cs[..., sl]
        shifted = jnp.pad(c, ((0, 0), (w, 0), (0, 0)))[:, :T]
        cnt = jnp.minimum(t + 1, w).astype(jnp.float32)
        mean = (c - shifted) / cnt[None, :, None]
        outs.append(mean - uf[..., sl])
    p = jnp.stack(outs, axis=2).astype(u.dtype)
    p = jnp.einsum('btgc,gcd->btgd', p, w_pool).reshape(B_, T, POOL_WIDTH)
    return p * pool_scale

def gla_chunked(q, k, v, log_a):
    B_, H, Tp, dk = q.shape
    dv = v.shape[-1]
    n = Tp // GLA_CHUNK

    def chunks(z):
        return jnp.moveaxis(z.reshape(B_, H, n, GLA_CHUNK, z.shape[-1]), 2, 0)

    mask = jnp.tril(jnp.ones((GLA_CHUNK, GLA_CHUNK), dtype=bool))[:, :, None]

    def step(S, xs):
        qc, kc, vc, gc = xs
        b = jnp.cumsum(gc, axis=2)
        o_inter = jnp.einsum('bhid,bhde->bhie', qc * jnp.exp(b), S)
        diff = b[:, :, :, None, :] - b[:, :, None, :, :]
        decay = jnp.where(mask, jnp.exp(jnp.where(mask, diff, 0.0)), 0.0)
        A = jnp.einsum('bhid,bhjd,bhijd->bhij', qc, kc, decay)
        o_intra = jnp.einsum('bhij,bhje->bhie', A, vc)
        b_last = b[:, :, -1:, :]
        S_new = S * jnp.exp(b_last[:, :, 0, :])[..., None] + jnp.einsum(
            'bhjd,bhje->bhde', kc * jnp.exp(b_last - b), vc)
        return S_new, o_inter + o_intra

    S0 = jnp.zeros((B_, H, dk, dv), jnp.float32)
    _, o = lax.scan(step, S0, (chunks(q), chunks(k), chunks(v), chunks(log_a)))
    return jnp.moveaxis(o, 0, 2).reshape(B_, H, Tp, dv)

def gla_mixer(q, k, v, r, g_lr, w_gate_up, b_gate, gla_norm_g):
    B_, T, _ = q.shape
    log_a = jax.nn.log_sigmoid((g_lr @ w_gate_up + b_gate).astype(jnp.float32)) / GLA_GATE_TEMP

    def heads(z, d):
        z = z.astype(jnp.float32).reshape(B_, T, GLA_HEADS, d).transpose(0, 2, 1, 3)
        return jnp.pad(z, ((0, 0), (0, 0), (GLA_PAD, 0), (0, 0)))

    qh = heads(q, GLA_DK) * (GLA_DK ** -0.5)
    kh = heads(k, GLA_DK)
    vh = heads(v, GLA_DV)
    gh = heads(log_a, GLA_DK)
    o = gla_chunked(qh, kh, vh, gh)[:, :, GLA_PAD:]
    o = o.transpose(0, 2, 1, 3)
    o = o * lax.rsqrt(jnp.mean(jnp.square(o), axis=-1, keepdims=True) + RMS_EPS)
    o = o.reshape(B_, T, GLA_WIDTH) * gla_norm_g.astype(jnp.float32)
    return (o * jax.nn.silu(r.astype(jnp.float32))).astype(q.dtype)

def setup_inputs(seed: int = 0) -> dict:
    key = jax.random.key(seed)
    ks = jax.random.split(key, 24)
    f32 = jnp.float32

    def nrm(k, shape, scale):
        return jax.random.normal(k, shape, f32) * scale

    L = DEPTH
    return {
        "x": nrm(ks[0], (BATCH, SEQ, D_MODEL), 1.0),
        "meta_tokens": nrm(ks[1], (N_META, D_MODEL), 1.0),
        "ffn1_w_gate": nrm(ks[2], (L, D_MODEL, D_FF), D_MODEL ** -0.5),
        "ffn1_w_up": nrm(ks[3], (L, D_MODEL, D_FF), D_MODEL ** -0.5),
        "ffn1_w_down": nrm(ks[4], (L, D_FF, D_MODEL), DEEPNORM_BETA * D_FF ** -0.5),
        "ln1_g": 1.0 + nrm(ks[5], (L, D_MODEL), 0.02),
        "ln1_b": nrm(ks[6], (L, D_MODEL), 0.02),
        "w_in": nrm(ks[7], (L, D_MODEL, IN_PROJ_COLS), D_MODEL ** -0.5),
        "w_gate_up": nrm(ks[8], (L, GLA_GATE_RANK, GLA_KEY_WIDTH), GLA_GATE_RANK ** -0.5),
        "b_gate": nrm(ks[9], (L, GLA_KEY_WIDTH), 0.1),
        "w_pool": nrm(ks[10], (L, POOL_GROUPS, POOL_GROUP_DIM, POOL_GROUP_DIM), POOL_GROUP_DIM ** -0.5),
        "pool_scale": 1.0 + nrm(ks[11], (L, POOL_WIDTH), 0.1),
        "gla_norm_g": 1.0 + nrm(ks[12], (L, GLA_WIDTH), 0.02),
        "w_out": nrm(ks[13], (L, MIX_WIDTH, D_MODEL), DEEPNORM_BETA * MIX_WIDTH ** -0.5),
        "ln2_g": 1.0 + nrm(ks[14], (L, D_MODEL), 0.02),
        "ln2_b": nrm(ks[15], (L, D_MODEL), 0.02),
        "ffn2_w_gate": nrm(ks[16], (L, D_MODEL, D_FF), D_MODEL ** -0.5),
        "ffn2_w_up": nrm(ks[17], (L, D_MODEL, D_FF), D_MODEL ** -0.5),
        "ffn2_w_down": nrm(ks[18], (L, D_FF, D_MODEL), DEEPNORM_BETA * D_FF ** -0.5),
        "ln3_g": 1.0 + nrm(ks[19], (L, D_MODEL), 0.02),
        "ln3_b": nrm(ks[20], (L, D_MODEL), 0.02),
    }

def reference(x, meta_tokens, ffn1_w_gate, ffn1_w_up, ffn1_w_down, ln1_g, ln1_b,
              w_in, w_gate_up, b_gate, w_pool, pool_scale, gla_norm_g, w_out,
              ln2_g, ln2_b, ffn2_w_gate, ffn2_w_up, ffn2_w_down, ln3_g, ln3_b):
    B_ = x.shape[0]
    meta = jnp.broadcast_to(meta_tokens[None].astype(x.dtype), (B_, N_META, D_MODEL))
    h = jnp.concatenate([meta, x], axis=1)
    a = DEEPNORM_ALPHA
    s0 = POOL_WIDTH
    s1 = s0 + GLA_KEY_WIDTH
    s2 = s1 + GLA_KEY_WIDTH
    s3 = s2 + GLA_WIDTH
    s4 = s3 + GLA_WIDTH
    for l in range(DEPTH):
        h = layer_norm(a * h + 0.5 * swiglu(h, ffn1_w_gate[l], ffn1_w_up[l], ffn1_w_down[l]),
                       ln1_g[l], ln1_b[l])
        z = h @ w_in[l]
        u_pool = z[..., :s0]
        q, k, v, r, g_lr = z[..., s0:s1], z[..., s1:s2], z[..., s2:s3], z[..., s3:s4], z[..., s4:]
        y_pool = pool_mixer(u_pool, w_pool[l], pool_scale[l])
        y_gla = gla_mixer(q, k, v, r, g_lr, w_gate_up[l], b_gate[l], gla_norm_g[l])
        y = jnp.concatenate([y_pool, y_gla], axis=-1) @ w_out[l]
        h = layer_norm(a * h + y, ln2_g[l], ln2_b[l])
        h = layer_norm(a * h + 0.5 * swiglu(h, ffn2_w_gate[l], ffn2_w_up[l], ffn2_w_down[l]),
                       ln3_g[l], ln3_b[l])
    return h[:, N_META:]


_drawn_inputs = setup_inputs


def setup_inputs(seed=0):
    import zlib

    import numpy as np

    out = dict(_drawn_inputs(seed))
    spreads = {}
    factors = {'b_gate': 6.077, 'gla_norm_g': 8.0}
    for name, (base, spread) in spreads.items():
        noise = np.random.default_rng([zlib.crc32(name.encode()), seed]).standard_normal(out[name].shape)
        drawn = base * np.exp(spread * noise) if base else spread * noise
        out[name] = __import__('jax').numpy.asarray(drawn.astype(out[name].dtype))
    for name, factor in factors.items():
        out[name] = (out[name] * factor).astype(out[name].dtype)
    return out
```

```python
from contextlib import ExitStack

import concourse.bass as bass
from concourse import mybir

F32 = mybir.dt.float32
F32R = mybir.dt.float32r
I32 = mybir.dt.int32
ALU = mybir.AluOpType
ACT = mybir.ActivationFunctionType

P = 128
D = 1024
SEQ = 512
DEPTH = 2
META = 16
T = SEQ + META
HALF = T // 2
KC = D // P
FF = 2816
MT = FF // P
PHASES = ((0, 8), (8, 8), (16, 6))
POOL_W = 512
GROUPS = 4
KEY_W = 256
HEADS = 4
DK = 64
DV = 128
RANK = 16
GATE_TEMP = 16.0
WINDOWS = (2, 4, 8, 16)
ALPHA = (2.0 * DEPTH) ** 0.25
LN_EPS = 1e-5
RMS_EPS = 1e-6

SLOTS = 4
RAWS = 2
TILES = 8
PIECE = TILES * P

CH = 128
NCH = SEQ // CH
TAIL = NCH * CH
LEVELS = (64, 32, 16, 8, 4, 2, 1)

FFN_PIECES = 2 * MT + len(PHASES) * KC
MIX_IN = 16
MIX_OUT = 8
LAYER_PIECES = 2 * FFN_PIECES + MIX_IN + MIX_OUT
IN_TILES = (4, 5, 6, 7, 8, 9, 10, 11, 0, 1, 2, 3, 12, 13, 14, 15)

C_LN = 0
C_BG = 48
C_PS = 50
C_GN = 54
C_WP = 64
C_GU = C_WP + GROUPS * P
C_GL = C_GU + KEY_W
C_ALL = C_GL + KC * RANK

STREAM = 36
DVE_MIX = 0
GROUPS_ORDER = ([("q", 0), ("q", 1), ("k", 0), ("k", 1)] + [("v", h) for h in range(4)]
                + [("u", 0), ("u", 1), ("w", 0), ("u", 2), ("w", 1), ("u", 3), ("w", 2), ("r", 0), ("w", 3),
                   ("r", 1), ("r", 2), ("r", 3)]
                + [("p", m) for m in range(8)] + [("g", m) for m in range(8)])


def gate_piece(l, f, m):
    phase = max(p for p, (m0, _) in enumerate(PHASES) if m0 <= m)
    return l * LAYER_PIECES + (f * (FFN_PIECES + MIX_IN + MIX_OUT) + 2 * m + KC * phase + 1)


def down_piece(l, f, p, mo):
    return l * LAYER_PIECES + (f * (FFN_PIECES + MIX_IN + MIX_OUT) + 2 * sum(PHASES[p]) + KC * p + mo + 1)


def stream_ready(l, idx):
    kind, n = GROUPS_ORDER[idx]
    if kind == "w":
        return "pw_acc", l * 4 + (n + 1)
    if kind in "pg":
        done = 4 * (kind == "g") + n // 2
        if n % 2 == 0:
            return "out_acc", l * 8 + (done + 1)
        return "piece_done", l * LAYER_PIECES + (FFN_PIECES + MIX_IN + done + 1)
    base = {"q": 0, "k": 2, "v": 4, "u": 8, "r": 12}[kind]
    return "piece_done", l * LAYER_PIECES + (FFN_PIECES + base + n + 1)


def build(nc, x_t, stream, params, out_t):
    ctx = ExitStack()
    with ctx:
        def sb(name, shape, dt=F32, where=ctx):
            return where.enter_context(nc.sbuf_tensor(name, shape, dt))

        def sem(name):
            return ctx.enter_context(nc.semaphore(name))

        raw = sb("raw", [P, RAWS, PIECE])
        w_hi = sb("w_hi", [P, SLOTS, PIECE], F32R)
        w_lo = sb("w_lo", [P, SLOTS, PIECE], F32R)
        X = sb("X", [P, KC, T])
        x_hi = sb("x_hi", [P, KC, T], F32R)
        x_lo = sb("x_lo", [P, KC, T], F32R)
        par = sb("par", [P, C_ALL])
        ones_mean = sb("ones_mean", [P, P])
        ones_rms = sb("ones_rms", [P, P])
        ident = sb("ident", [P, P])
        ident_mask = sb("ident_mask", [P, P], I32)
        level_mask = sb("level_mask", [P, len(LEVELS), CH // 2], I32)
        chunk_mask = sb("chunk_mask", [P, T])
        inv_count = sb("inv_count", [P, META])
        ln_eps = sb("ln_eps", [P, 1])
        rms_eps = sb("rms_eps", [P, 1])
        acc_a = sb("acc_a", [P, HEADS, NCH, CH])
        acc_t = sb("acc_t", [META, HEADS, META])
        with ExitStack() as s1:
            sum_x = sb("sum_x", [P, T], F32, s1)
            sum_sq = sb("sum_sq", [P, T], F32, s1)
            sq = sb("sq", [P, 2, T], F32, s1)
            mean_sq = sb("mean_sq", [P, T], F32, s1)
            var = sb("var", [P, T], F32, s1)
            rstd = sb("rstd", [P, T], F32, s1)
            mean_rstd = sb("mean_rstd", [P, T], F32, s1)
            xhat = sb("xhat", [P, 2, T], F32, s1)
        with ExitStack() as s2:
            ex = sb("ex", [P, 4, T], F32, s2)
            kt = sb("kt", [P, 2, 2, T], F32, s2)
            qt = sb("qt", [P, 2, 2, HALF], F32, s2)
        sb("reserve_ln", [P, 10 * T])
        with ExitStack() as s3:
            h_hi = sb("h_hi", [P, TILES, T], F32R, s3)
            h_lo = sb("h_lo", [P, TILES, T], F32R, s3)
            silu = sb("silu", [P, T], F32, s3)
            prod = sb("prod", [P, T], F32, s3)
        yp_hi = sb("yp_hi", [P, GROUPS, T], F32R)
        yp_lo = sb("yp_lo", [P, GROUPS, T], F32R)
        qk = sb("qk", [P, 4, T])
        bcum = sb("bcum", [P, 2, T])
        kdec = sb("kdec", [P, 2, SEQ])
        qe = sb("qe", [P, 2, T])
        elast = sb("elast", [P, 2, NCH])
        ft = sb("ft", [P, 2, T])
        win = sb("win", [P, 2, T])
        v_tok = sb("v_tok", [P, HEADS, NCH, DV])
        v_tail = sb("v_tail", [META, HEADS, DV])
        kd_tok = sb("kd_tok", [P, 2, NCH, CH])
        state = sb("state", [P, 2, NCH, DV])
        s_r = sb("s_r", [P, HEADS, T])
        glr = sb("glr", [RANK, T])

        PS = [ctx.enter_context(nc.psum_tensor(f"PS{i}", [P, 2, 512], F32)) for i in range(4)]

        def pair(i):
            return PS[i][:, :, 0:HALF]

        def halves(ap):
            return ap.rearrange("p (a b) -> p a b", a=2)

        names = """x_loaded par_loaded consts consts_dve masks raw_hi split_done piece_done out_stored setup row_sync
            silu_done prod_done h_hi_done h_lo_done down_evac
            resid_done sq_done s1_done s2_done mean_acc msq_acc mean_sq_done var_done std_done rstd_done mr_done
            xmul_done xhat_done x_hi_done x_full_done x_lo_done init_hi
            pw_acc out_acc qkv_evac u_evac w_evac sr_evac wop_evac glr_acc glr_done z_acc zb_done abs_done en_done
            ln_done b_step b_done arg_step arg_done exp_done qe_done kdec_done ktqt_step ktqt_done lev_acc lev_evac
            diag_acc diag_evac tdiag_acc tdiag_evac vtr_acc v_tok_done v_tail_done ktr_acc kd_tok_done
            u_acc s_step s_done pool_step pool_done wsplit_step o_acc o_done osq_done ms_acc rms_std o_step o_fin
            o_hi_done o_lo_done acc_zero""".split()
        S = {n: sem(n) for n in names}
        raw_full = [sem(f"raw_full{i}") for i in range(RAWS)]
        block = ctx.enter_context(nc.Block())

        LN_PER = 3

        def wait_stream(eng, l, idx):
            name, value = stream_ready(l, idx)
            eng.wait_ge(S[name], value)

        @block.sync
        def _(sp):
            for k in range(KC):
                sp.dma_start(X[:, k, :], x_t[k * P:(k + 1) * P, :]).then_inc(S["x_loaded"], 16)
            for n in range(RAWS):
                sp.dma_start(raw[:, n, :], stream[0, n]).then_inc(raw_full[n], 16)
            with sp.Fori(1, DEPTH * LAYER_PIECES // RAWS) as i:
                for n in range(RAWS):
                    sp.wait_ge(S["split_done"], i * RAWS + (n - RAWS + 1))
                    sp.dma_start(raw[:, n, :], stream[i, n]).then_inc(raw_full[n], 16)
            for k in range(KC):
                sp.wait_ge(S["x_full_done"], DEPTH * LN_PER * KC - KC + k + 1)
                sp.dma_start(out_t[k * P:(k + 1) * P, :], X[:, k, META:T]).then_inc(S["out_stored"], 16)
            sp.wait_ge(S["out_stored"], 16 * KC)

        @block.gpsimd
        def _(pool):
            def split(slot, full, free, done):
                r = slot % RAWS
                pool.wait_ge(S["masks"], 1)
                pool.wait_ge(raw_full[r], full)
                if free is not None:
                    pool.wait_ge(S["piece_done"], free)
                pool.wait_ge(S["split_done"], done)
                nc.gpsimd.tensor_copy(w_hi[:, slot, :], raw[:, r, :]).then_inc(S["raw_hi"], 1)

            def split_rest(slot, done):
                r = slot % RAWS
                pool.wait_ge(S["raw_hi"], done)
                nc.gpsimd.tensor_tensor(w_lo[:, slot, :], raw[:, r, :], w_hi[:, slot, :].bitcast(F32),
                                        ALU.subtract).then_inc(S["split_done"], 1)

            nc.gpsimd.memset(level_mask[:, :, :], 1).then_inc(S["consts"], 1)
            nc.gpsimd.memset(ident_mask[:, :], 0).then_inc(S["consts"], 1)
            nc.gpsimd.memset(ident[:, :], 0.0).then_inc(S["consts"], 1)
            pool.wait_ge(S["consts"], 3)
            n = 3
            for m in (ident_mask, ident):
                nc.gpsimd.affine_select(out=m[:, :], in_=m[:, :], compare_op=ALU.not_equal, fill=1.0, base=0,
                                        pattern=[[-1, P]], channel_multiplier=1).then_inc(S["consts"], 1)
            n += 2
            for i, s in enumerate(LEVELS):
                m = level_mask[:, i, :].rearrange("p (b s) -> p b s", s=s)
                nb = CH // 2 // s
                nc.gpsimd.affine_select(out=m, in_=m, compare_op=ALU.is_ge, fill=0.0, base=0,
                                        pattern=[[-2 * s, nb], [0, s]], channel_multiplier=1).then_inc(S["consts"], 1)
                n += 1
                pool.wait_ge(S["consts"], n)
                nc.gpsimd.affine_select(out=m, in_=m, compare_op=ALU.is_ge, fill=0.0, base=s - 1,
                                        pattern=[[2 * s, nb], [0, s]], channel_multiplier=-1).then_inc(S["consts"], 1)
                n += 1
                pool.wait_ge(S["consts"], n)
            nc.gpsimd.memset(acc_t[:, :, :], 0.0).then_inc(S["masks"], 1)
            for n in range(SLOTS):
                split(n, 16 * (n // RAWS + 1), None, n)
                split_rest(n, n + 1)
            full, free, done = (pool.alloc_register(r) for r in ("full", "free", "done"))
            pool.reg_mov(full, 16 * (SLOTS // RAWS))
            pool.reg_mov(free, 0)
            pool.reg_mov(done, SLOTS)
            with pool.Fori(1, DEPTH * LAYER_PIECES // SLOTS):
                for n in range(SLOTS):
                    if n % RAWS == 0:
                        pool.reg_add(full, full, 16)
                    pool.reg_add(free, free, 1)
                    split(n, full, free, done)
                    pool.reg_add(done, done, 1)
                    split_rest(n, done)

        @block.tensor
        def _(pe):
            def tile_products(ps, slot, t, k, rhs_hi, rhs_lo, first, last, half):
                hi = w_hi[:, slot, t * P:(t + 1) * P]
                lo = w_lo[:, slot, t * P:(t + 1) * P]
                tok = slice(half * HALF, (half + 1) * HALF)
                o = PS[ps][:, half, 0:HALF]
                nc.tensor.matmul(o, hi, rhs_hi[:, k, tok], start=first, stop=False)
                nc.tensor.matmul(o, hi, rhs_lo[:, k, tok], start=False, stop=False)
                return nc.tensor.matmul(o, lo, rhs_hi[:, k, tok], start=False, stop=last)

            def product(ps, slot, rhs_hi, rhs_lo, n, t0=0, k0=0):
                for k in range(n):
                    for half in range(2):
                        m = tile_products(ps, slot, t0 + k, k0 + k, rhs_hi, rhs_lo, k == 0, k == n - 1, half)
                return m

            def ffn(l, f):
                F22, FP, FD = l * 44 + 22 * f, l * LAYER_PIECES + f * (FFN_PIECES + MIX_IN + MIX_OUT), \
                    l * 32 + 16 * f
                LN = l * LN_PER + 2 * f
                piece = 0
                for p, (m0, nm) in enumerate(PHASES):
                    last_phase = p == len(PHASES) - 1
                    prev = 16 * 0

                    def gate_up(i, first, base):
                        for j in range(4):
                            m = i * 2 + (m0 + j // 2)
                            pe.wait_ge(S["split_done"], FP + i * 4 + (base + j + 1))
                            if not first:
                                pe.wait_ge(S["silu_done" if j % 2 == 0 else "prod_done"], F22 + m - 1)
                            elif p > 0:
                                pe.wait_ge(S["down_evac"], FD + (8 * (p - 1) + 4 + j + 1))
                            product(j, j, x_hi, x_lo, KC).then_inc(S["piece_done"], 1)

                    if p == 0:
                        for j in range(3):
                            pe.wait_ge(S["split_done"], FP + (j + 1))
                        for k in range(KC):
                            pe.wait_ge(S["x_lo_done"], LN * KC + (k + 1))
                            for j in range(3):
                                for half in range(2):
                                    m = tile_products(j, j, k, k, x_hi, x_lo, k == 0, k == KC - 1, half)
                                if k == KC - 1:
                                    m.then_inc(S["piece_done"], 1)
                        pe.wait_ge(S["split_done"], FP + 4)
                        product(3, 3, x_hi, x_lo, KC).then_inc(S["piece_done"], 1)
                    else:
                        gate_up(0, True, piece)
                    with pe.Fori(1, nm // 2) as i:
                        gate_up(i, False, piece)
                    piece += 2 * nm
                    for mo in range(KC):
                        j = mo % 4
                        pe.wait_ge(S["split_done"], FP + (piece + mo + 1))
                        if mo < 4:
                            pe.wait_ge(S["silu_done" if j % 2 == 0 else "prod_done"],
                                       F22 + (m0 + nm - 1 + mo // 2))
                        elif last_phase:
                            pe.wait_ge(S["resid_done"], LN * KC + (mo - 3))
                        else:
                            pe.wait_ge(S["down_evac"], FD + (8 * p + mo - 3))
                        for k in range(nm):
                            if mo == 0:
                                pe.wait_ge(S["h_lo_done"], F22 + (m0 + k + 1))
                            for half in range(2):
                                m = tile_products(j, (piece + mo) % 4, k, k, h_hi, h_lo, k == 0, k == nm - 1, half)
                        m.then_inc(S["piece_done"], 1)
                    piece += KC

            def ln_stats(LN):
                pe.wait_ge(S["s1_done"], LN * 7 + 7)
                for half in range(2):
                    m = nc.tensor.matmul(PS[0][:, half, 0:HALF], ones_mean[:, :], sum_x[:, half * HALF:(half + 1) * HALF],
                                         start=True, stop=True)
                m.then_inc(S["mean_acc"], 1)
                pe.wait_ge(S["s2_done"], LN * 7 + 7)
                for half in range(2):
                    m = nc.tensor.matmul(PS[1][:, half, 0:HALF], ones_mean[:, :],
                                         sum_sq[:, half * HALF:(half + 1) * HALF], start=True, stop=True)
                m.then_inc(S["msq_acc"], 1)

            def group_free(l, idx):
                kind, n = GROUPS_ORDER[idx]
                at = {"q": ("qkv_evac", 8, n), "k": ("qkv_evac", 8, 2 + n), "v": ("qkv_evac", 8, 4 + n),
                      "u": ("u_evac", 4, n), "w": ("w_evac", 4, n), "r": ("sr_evac", 4, n),
                      "p": ("wop_evac", 8, n)}.get(kind)
                if kind == "g":
                    pe.wait_ge(S["resid_done"], l * 24 + (8 + n + 1))
                else:
                    pe.wait_ge(S[at[0]], l * at[1] + (at[2] + 1))

            def mixer(l):
                FP = l * LAYER_PIECES + FFN_PIECES
                LN = l * LN_PER + 1
                for j in range(2):
                    pe.wait_ge(S["split_done"], FP + (j + 1))
                pe.wait_ge(S["par_loaded"], l * 16 + 16)
                for k in range(KC):
                    pe.wait_ge(S["x_lo_done"], LN * KC + (k + 1))
                    for j in range(2):
                        for half in range(2):
                            m = tile_products(j, j, k, k, x_hi, x_lo, k == 0, k == KC - 1, half)
                        if k == KC - 1:
                            m.then_inc(S["piece_done"], 1)
                    for half in range(2):
                        m = nc.tensor.matmul(PS[2][0:RANK, half, 0:HALF], par[:, C_GL + k * RANK:C_GL + (k + 1) * RANK],
                                             X[:, k, half * HALF:(half + 1) * HALF], start=k == 0, stop=k == KC - 1)
                m.then_inc(S["glr_acc"], 1)
                pieces = [2]

                def project(idx):
                    pe.wait_ge(S["split_done"], FP + (pieces[0] + 1))
                    group_free(l, idx - 2)
                    product(idx % 2, pieces[0] % 4, x_hi, x_lo, KC).then_inc(S["piece_done"], 1)
                    pieces[0] += 1

                def pool_product(idx, g):
                    pe.wait_ge(S["pool_done"], l * 4 + (g + 1))
                    group_free(l, idx - 2)
                    for half in range(2):
                        m = nc.tensor.matmul(PS[idx % 2][:, half, 0:HALF], par[:, C_WP + g * P:C_WP + (g + 1) * P],
                                             ft[:, g % 2, half * HALF:(half + 1) * HALF], start=True, stop=True)
                    m.then_inc(S["pw_acc"], 1)

                def gate_logits():
                    pe.wait_ge(S["glr_done"], l + 1)
                    for t in range(2):
                        for half in range(2):
                            m = nc.tensor.matmul(PS[2 + t][:, half, 0:HALF],
                                                 par[0:RANK, C_GU + t * P:C_GU + (t + 1) * P],
                                                 glr[:, half * HALF:(half + 1) * HALF], start=True, stop=True)
                        m.then_inc(S["z_acc"], 1)

                def rows(h):
                    return slice((h % 2) * DK, (h % 2 + 1) * DK)

                def even_tails(product):
                    product(0)
                    product(2).then_inc(S["row_sync"], 1)

                def odd_tails(product):
                    product(1)
                    return product(3)

                def diagonal():
                    pe.wait_ge(S["qkv_evac"], l * 8 + 4)
                    pe.wait_ge(S["zb_done"], l * 2 + 2)
                    for h in range(HEADS):
                        for c in range(NCH):
                            tok = slice(c * CH, (c + 1) * CH)
                            m = nc.tensor.matmul(PS[2 + h % 2][:, h // 2, tok], qk[rows(h), 2 + h // 2, tok],
                                                 qk[rows(h), h // 2, tok], start=True, stop=True)
                    m.then_inc(S["diag_acc"], 1)

                def tail_diagonal(h):
                    return nc.tensor.matmul(PS[3][0:META, 0, place(h) * META:(place(h) + 1) * META],
                                            qk[rows(h), 2 + h // 2, TAIL:T], qk[rows(h), h // 2, TAIL:T],
                                            start=True, stop=True)

                def v_transpose(h):
                    pe.wait_ge(S["qkv_evac"], l * 8 + (4 + h + 1))
                    if h > 0:
                        pe.wait_ge(S["v_tok_done"], l * 4 + h)
                        pe.wait_ge(S["v_tail_done"], l * 4 + h)
                    for c in range(NCH):
                        nc.tensor.transpose(PS[3][:, 1, c * CH:(c + 1) * CH], ft[:, h % 2, c * CH:(c + 1) * CH], ident[:, :])
                    nc.tensor.transpose(PS[3][0:META, 0, 256:256 + DV], ft[:, h % 2, TAIL:T],
                                        ident[:, :]).then_inc(S["vtr_acc"], 1)

                def k_transpose(t):
                    pe.wait_ge(S["kdec_done"], l + 1)
                    if t == 0:
                        pe.wait_ge(S["v_tok_done"], l * 4 + 4)
                    else:
                        pe.wait_ge(S["kd_tok_done"], l * 2 + 1)
                    for c in range(NCH):
                        m = nc.tensor.transpose(PS[3][:, 1, c * CH:(c + 1) * CH], kdec[:, t, c * CH:(c + 1) * CH], ident[:, :])
                    m.then_inc(S["ktr_acc"], 1)

                def level(i):
                    s = LEVELS[i]
                    if i == 0:
                        pe.wait_ge(S["diag_evac"], l * 2 + 2)
                    else:
                        pe.wait_ge(S["lev_evac"], l * 7 + i)
                    if s <= META // 2:
                        pe.wait_ge(S["v_tail_done"], l * 4 + 4)
                    pe.wait_ge(S["ktqt_done"], l * 7 + (i + 1))
                    tail = s <= META // 2

                    def tail_level(h):
                        return nc.tensor.matmul(PS[3][0:META, 0, place(h) * 8:(place(h) + 1) * 8],
                                                kt[rows(h), i % 2, h // 2, TAIL:T], qt[rows(h), i % 2, h // 2, 256:264],
                                                start=True, stop=True)

                    for h in range(HEADS):
                        if tail and h == 1:
                            even_tails(tail_level)
                        for c in range(NCH):
                            if tail and h == 1 and c == 0:
                                pe.wait_ge(S["row_sync"], l * 5 + (i - 1))
                            m = nc.tensor.matmul(PS[2][:, h % 2, (h // 2) * 256 + c * 64:(h // 2) * 256 + (c + 1) * 64],
                                                 kt[rows(h), i % 2, h // 2, c * CH:(c + 1) * CH],
                                                 qt[rows(h), i % 2, h // 2, c * 64:(c + 1) * 64], start=True, stop=True)
                    if tail:
                        m = odd_tails(tail_level)
                    m.then_inc(S["lev_acc"], 1)

                def chunk_updates(t):
                    pe.wait_ge(S["kd_tok_done"], l * 2 + 2)
                    if t == 1:
                        pe.wait_ge(S["s_done"], l * 2 + 1)
                    pe.wait_ge(S["consts_dve"], 1)
                    for h in (2 * t, 2 * t + 1):
                        for c in range(NCH):
                            m = nc.tensor.matmul(PS[3][rows(h), 1, c * DV:(c + 1) * DV], kd_tok[:, t, c, rows(h)],
                                                 v_tok[:, h, c, :], start=True, stop=True)
                    m.then_inc(S["u_acc"], 1)

                def attend(h):
                    ps = 2 + h % 2
                    if h < 2:
                        pe.wait_ge(S["lev_evac"], l * 7 + 7)
                        pe.wait_ge(S["s_done"], l * 2 + 2)
                    else:
                        pe.wait_ge(S["o_done"], l * 4 + (h - 1))
                    for c in range(NCH):
                        tok = slice(c * CH, (c + 1) * CH)
                        if c > 0:
                            nc.tensor.matmul(PS[ps][:, 0, tok], state[rows(h), h // 2, c - 1, :], qe[rows(h), h // 2, tok],
                                             start=True, stop=False)
                        nc.tensor.matmul(PS[ps][:, 0, tok], v_tok[:, h, c, :], acc_a[:, place(h), c, :], start=c == 0, stop=True)
                    nc.tensor.matmul(PS[ps][:, 1, 0:META], state[rows(h), h // 2, NCH - 1, :], qe[rows(h), h // 2, TAIL:T],
                                     start=True, stop=False)
                    nc.tensor.matmul(PS[ps][:, 1, 0:META], v_tail[:, h, :], acc_t[:, place(h), :], start=False,
                                     stop=True).then_inc(S["o_acc"], 1)

                def rms(h):
                    pe.wait_ge(S["osq_done"], l * 4 + (h + 1))
                    if h < 2:
                        pe.wait_ge(S["o_done"], l * 4 + (h + 3))
                    else:
                        pe.wait_ge(S["rms_std"], l * 4 + (h - 1))
                    for half in range(2):
                        m = nc.tensor.matmul(PS[2 + h % 2][:, half, 0:HALF], ones_rms[:, :],
                                             ex[:, h, half * HALF:(half + 1) * HALF], start=True, stop=True)
                    m.then_inc(S["ms_acc"], 1)

                def out_product(idx, mo, part, rhs_hi, rhs_lo):
                    piece = MIX_IN + part * 4 + mo // 2
                    if mo % 2 == 0:
                        pe.wait_ge(S["split_done"], FP + (piece + 1))
                    group_free(l, idx - 2)
                    m = product(idx % 2, piece % 4, rhs_hi, rhs_lo, 4, 4 * (mo % 2))
                    m.then_inc(S["out_acc" if mo % 2 == 0 else "piece_done"], 1)

                project(2)
                gate_logits()
                project(3)
                project(4)
                diagonal()
                project(5)
                pe.wait_ge(S["masks"], 1)
                pe.wait_ge(S["diag_evac"], l * 2 + 2)
                even_tails(tail_diagonal)
                pe.wait_ge(S["row_sync"], l * 5 + 1)
                v_transpose(0)
                odd_tails(tail_diagonal).then_inc(S["tdiag_acc"], 1)
                project(6)
                level(0)
                v_transpose(1)
                project(7)
                level(1)
                v_transpose(2)
                project(8)
                level(2)
                v_transpose(3)
                project(9)
                pool_product(10, 0)
                level(3)
                k_transpose(0)
                project(11)
                pool_product(12, 1)
                level(4)
                k_transpose(1)
                project(13)
                pool_product(14, 2)
                level(5)
                project(15)
                pool_product(16, 3)
                level(6)
                chunk_updates(0)
                project(17)
                chunk_updates(1)
                project(18)
                attend(0)
                attend(1)
                project(19)
                attend(2)
                attend(3)
                pe.wait_ge(S["w_evac"], l * 4 + 4)
                for mo in range(8):
                    out_product(20 + mo, mo, 0, yp_hi, yp_lo)
                    if mo in (1, 3):
                        rms(mo - 1)
                        rms(mo)
                pe.wait_ge(S["o_lo_done"], l * 4 + 4)
                for mo in range(8):
                    out_product(28 + mo, mo, 1, x_hi, x_lo)

            pe.wait_ge(S["masks"], 1)
            pe.wait_ge(S["consts_dve"], 1)
            with pe.Fori(0, DEPTH) as l:
                ffn(l, 0)
                ln_stats(l * LN_PER)
                mixer(l)
                ln_stats(l * LN_PER + 1)
                ffn(l, 1)
                ln_stats(l * LN_PER + 2)

        @block.scalar
        def _(act):
            def ffn(l, f):
                F22 = l * 44 + 22 * f
                for m in range(MT):
                    act.wait_ge(S["piece_done"], gate_piece(l, f, m))
                    nc.scalar.activation(halves(silu[:, :]), pair(2 * (m % 2)), ACT.Silu).then_inc(S["silu_done"], 1)
                    act.wait_ge(S["prod_done"], F22 + (m + 1))
                    ph = max(p for p, (m0, _) in enumerate(PHASES) if m0 <= m)
                    nc.scalar.activation(h_hi[:, m - PHASES[ph][0], :], prod[:, :], ACT.Copy).then_inc(S["h_hi_done"], 1)
                squares(l * LN_PER + 2 * f)

            def squares(LN):
                for k in range(KC):
                    act.wait_ge(S["resid_done"], LN * KC + (k + 1))
                    if k >= 2:
                        act.wait_ge(S["s2_done"], LN * 7 + (k - 1 if k > 2 else 1))
                    nc.scalar.activation(sq[:, k % 2, :], X[:, k, :], ACT.Square).then_inc(S["sq_done"], 1)

            def norm(LN, r):
                act.wait_ge(S["mean_acc"], LN + 1)
                nc.scalar.activation(halves(mean_sq[:, :]), pair(0), ACT.Square).then_inc(S["mean_sq_done"], 1)
                act.wait_ge(S["var_done"], LN + 1)
                nc.scalar.activation(mean_sq[:, :], var[:, :], ACT.Sqrt).then_inc(S["std_done"], 1)
                g = C_LN + 16 * r
                for k in range(KC):
                    act.wait_ge(S["xhat_done"], LN * KC + (k + 1))
                    nc.scalar.activation(x_hi[:, k, :], xhat[:, k % 2, :], ACT.Identity, bias=par[:, g + 8 + k:g + 9 + k],
                                         scale=par[:, g + k:g + k + 1]).then_inc(S["x_hi_done"], 1)
                    nc.scalar.activation(X[:, k, :], xhat[:, k % 2, :], ACT.Identity, bias=par[:, g + 8 + k:g + 9 + k],
                                         scale=par[:, g + k:g + k + 1]).then_inc(S["x_full_done"], 1)

            def mixer(l):
                def evac(idx, out, scale=1.0):
                    wait_stream(act, l, idx)
                    nc.scalar.activation(halves(out), pair(idx % 2), ACT.Copy, scale=scale).then_inc(S["qkv_evac"], 1)

                def exp_of(i):
                    act.wait_ge(S["arg_done"], l * 8 + (i + 2))
                    e = ex[:, 2 * (i % 2):2 * (i % 2) + 2, :] if LEVELS[i] <= META // 2 else \
                        ex[:, 2 * (i % 2):2 * (i % 2) + 2, 0:SEQ]
                    nc.scalar.activation(e, e, ACT.Exp, scale=1.0 / GATE_TEMP).then_inc(S["exp_done"], 1)

                def v_to_tokens(h):
                    act.wait_ge(S["vtr_acc"], l * 4 + (h + 1))
                    nc.scalar.activation(v_tok[:, h, :, :].rearrange("p c d -> p (c d)"), PS[3][:, 1, :],
                                         ACT.Copy).then_inc(S["v_tok_done"], 1)

                def k_to_tokens(t):
                    act.wait_ge(S["ktr_acc"], l * 2 + (t + 1))
                    nc.scalar.activation(kd_tok[:, t, :, :].rearrange("p c d -> p (c d)"), PS[3][:, 1, :],
                                         ACT.Copy).then_inc(S["kd_tok_done"], 1)

                evac(0, qk[:, 0, :], DK ** -0.5)
                evac(1, qk[:, 1, :], DK ** -0.5)
                evac(2, qk[:, 2, :])
                for t in range(2):
                    act.wait_ge(S["z_acc"], l * 2 + (t + 1))
                    nc.scalar.activation(halves(bcum[:, t, :]), pair(2 + t), ACT.Identity,
                                         bias=par[:, C_BG + t:C_BG + t + 1]).then_inc(S["zb_done"], 1)
                act.wait_ge(S["abs_done"], l + 1)
                nc.scalar.activation(ex[:, 0:2, :], ex[:, 0:2, :], ACT.Exp, scale=-1.0).then_inc(S["en_done"], 1)
                act.wait_ge(S["en_done"], l + 1)
                nc.scalar.activation(ex[:, 0:2, :], ex[:, 0:2, :], ACT.Ln, bias=1.0).then_inc(S["ln_done"], 1)
                evac(3, qk[:, 3, :])
                act.wait_ge(S["b_done"], l + 1)
                nc.scalar.activation(ex[:, 0:2, :], bcum[:, :, :], ACT.Exp, scale=1.0 / GATE_TEMP).then_inc(S["exp_done"], 1)
                act.wait_ge(S["arg_done"], l * 8 + 1)
                nc.scalar.activation(ex[:, 2:4, 0:SEQ], ex[:, 2:4, 0:SEQ], ACT.Exp,
                                     scale=1.0 / GATE_TEMP).then_inc(S["exp_done"], 1)
                evac(4, ft[:, 0, :])
                exp_of(0)
                evac(5, ft[:, 1, :])
                exp_of(1)
                v_to_tokens(0)
                exp_of(2)
                evac(6, ft[:, 0, :])
                v_to_tokens(1)
                exp_of(3)
                evac(7, ft[:, 1, :])
                v_to_tokens(2)
                exp_of(4)
                v_to_tokens(3)
                exp_of(5)
                k_to_tokens(0)
                exp_of(6)
                k_to_tokens(1)
                for h, idx in enumerate((15, 17, 18, 19)):
                    wait_stream(act, l, idx)
                    nc.scalar.activation(halves(s_r[:, h, :]), pair(idx % 2), ACT.Silu).then_inc(S["sr_evac"], 1)
                for h in range(HEADS):
                    act.wait_ge(S["o_done"], l * 4 + (h + 1))
                    nc.scalar.activation(ex[:, h, :], qk[:, h, :], ACT.Square).then_inc(S["osq_done"], 1)
                for h in range(HEADS):
                    act.wait_ge(S["ms_acc"], l * 4 + (h + 1))
                    nc.scalar.activation(halves(ex[:, h, :]), pair(2 + h % 2), ACT.Sqrt,
                                         bias=rms_eps[:, :]).then_inc(S["rms_std"], 1)
                for h in range(HEADS):
                    act.wait_ge(S["o_fin"], l * 4 + (h + 1))
                    nc.scalar.activation(x_hi[:, h, :], qk[:, h, :], ACT.Copy).then_inc(S["o_hi_done"], 1)
                squares(l * LN_PER + 1)

            act.dma_start(par[:, :], params[0]).then_inc(S["par_loaded"], 16)
            for k in range(KC):
                act.wait_ge(S["x_loaded"], 16 * KC)
                nc.scalar.activation(x_hi[:, k, :], X[:, k, :], ACT.Copy).then_inc(S["init_hi"], 1)
            act.wait_ge(S["consts_dve"], 1)
            act.wait_ge(S["par_loaded"], 16)
            with act.Fori(0, DEPTH) as l:
                ffn(l, 0)
                norm(l * LN_PER, 0)
                mixer(l)
                norm(l * LN_PER + 1, 1)
                ffn(l, 1)
                norm(l * LN_PER + 2, 2)
                act.wait_ge(S["x_full_done"], l * 24 + 24)
                act.dma_start(par[:, :], params[l + 1]).then_inc(S["par_loaded"], 16)
                act.wait_ge(S["par_loaded"], l * 16 + 32)

        @block.vector
        def _(dve):
            V = nc.vector

            def ffn(l, f):
                F22 = l * 44 + 22 * f
                down = 0
                FD = l * 48 + 24 * f
                for p, (m0, nm) in enumerate(PHASES):
                    for m in range(m0, m0 + nm):
                        dve.wait_ge(S["silu_done"], F22 + (m + 1))
                        dve.wait_ge(S["piece_done"], gate_piece(l, f, m) + 1)
                        if m > 0:
                            dve.wait_ge(S["h_lo_done"], F22 + m)
                        V.scalar_tensor_tensor(out=halves(prod[:, :]), in0=pair(2 * (m % 2) + 1), scalar=0.5,
                                               in1=halves(silu[:, :]), op0=ALU.mult, op1=ALU.mult).then_inc(S["prod_done"], 1)
                        dve.wait_ge(S["h_hi_done"], F22 + (m + 1))
                        V.tensor_tensor(h_lo[:, m - m0, :], prod[:, :], h_hi[:, m - m0, :].bitcast(F32),
                                        ALU.subtract).then_inc(S["h_lo_done"], 1)
                    if p == len(PHASES) - 1:
                        resid(l * LN_PER + 2 * f, lambda mo: ("piece_done", down_piece(l, f, p, mo)), 4)
                        break
                    for mo in range(KC):
                        dve.wait_ge(S["piece_done"], down_piece(l, f, p, mo))
                        if p == 0:
                            V.scalar_tensor_tensor(out=halves(X[:, mo, :]), in0=halves(X[:, mo, :]), scalar=ALPHA,
                                                   in1=pair(mo % 4), op0=ALU.mult, op1=ALU.add).then_inc(S["down_evac"], 1)
                        else:
                            dve.wait_ge(S["down_evac"], l * 32 + 16 * f + 8)
                            V.tensor_tensor(halves(X[:, mo, :]), halves(X[:, mo, :]), pair(mo % 4),
                                            ALU.add).then_inc(S["down_evac"], 1)

            def resid(LN, ready, pairs):
                def add_square(k):
                    dve.wait_ge(S["sq_done"], LN * KC + (k + 1))
                    if k == 1:
                        V.tensor_tensor(sum_sq[:, :], sq[:, 0, :], sq[:, 1, :], ALU.add).then_inc(S["s2_done"], 1)
                    elif k > 1:
                        dve.wait_ge(S["s2_done"], LN * 7 + (k - 1))
                        V.tensor_tensor(sum_sq[:, :], sum_sq[:, :], sq[:, k % 2, :], ALU.add).then_inc(S["s2_done"], 1)

                for mo in range(KC):
                    name, value = ready(mo)
                    dve.wait_ge(S[name], value)
                    V.tensor_tensor(halves(X[:, mo, :]), halves(X[:, mo, :]), pair(mo % pairs),
                                    ALU.add).then_inc(S["resid_done"], 1)
                    if mo >= 1:
                        add_square(mo - 1)
                        dve.wait_ge(S["resid_done"], LN * KC + (mo + 1))
                        if mo > 1:
                            dve.wait_ge(S["s1_done"], LN * 7 + (mo - 1))
                        V.tensor_tensor(sum_x[:, :], X[:, 0, :] if mo == 1 else sum_x[:, :], X[:, mo, :],
                                        ALU.add).then_inc(S["s1_done"], 1)
                add_square(KC - 1)

            def norm(LN):
                dve.wait_ge(S["mean_sq_done"], LN + 1)
                dve.wait_ge(S["msq_acc"], LN + 1)
                V.scalar_tensor_tensor(out=halves(var[:, :]), in0=pair(1), scalar=LN_EPS, in1=halves(mean_sq[:, :]),
                                       op0=ALU.add, op1=ALU.subtract).then_inc(S["var_done"], 1)
                dve.wait_ge(S["std_done"], LN + 1)
                V.reciprocal(rstd[:, :], mean_sq[:, :]).then_inc(S["rstd_done"], 1)
                dve.wait_ge(S["rstd_done"], LN + 1)
                V.tensor_tensor(halves(mean_rstd[:, :]), pair(0), halves(rstd[:, :]), ALU.mult).then_inc(S["mr_done"], 1)

                def lo(k):
                    dve.wait_ge(S["x_full_done"], LN * KC + (k + 1))
                    V.tensor_tensor(x_lo[:, k, :], X[:, k, :], x_hi[:, k, :].bitcast(F32),
                                    ALU.subtract).then_inc(S["x_lo_done"], 1)

                for k in range(KC):
                    V.tensor_tensor(xhat[:, k % 2, :], X[:, k, :], rstd[:, :], ALU.mult).then_inc(S["xmul_done"], 1)
                    if k == 0:
                        dve.wait_ge(S["mr_done"], LN + 1)
                    dve.wait_ge(S["xmul_done"], LN * KC + (k + 1))
                    V.tensor_tensor(xhat[:, k % 2, :], xhat[:, k % 2, :], mean_rstd[:, :],
                                    ALU.subtract).then_inc(S["xhat_done"], 1)
                    if k >= 1:
                        lo(k - 1)
                lo(KC - 1)

            def mixer(l):
                pair_exp = [ex[:, 0:2, :], ex[:, 2:4, :]]
                steps = {"pool": 0, "kq": 0, "arg": 0}

                def step(name, total, ins):
                    steps[name] = steps.get(name, 0) + 1
                    ins.then_inc(S[name], 1)
                    dve.wait_ge(S[name], l * total + steps[name])

                dve.wait_ge(S["glr_acc"], l + 1)
                V.tensor_copy(halves(glr[:, :]), PS[2][0:RANK, :, 0:HALF]).then_inc(S["glr_done"], 1)
                V.memset(acc_a[:, :, :, :], 0.0).then_inc(S["acc_zero"], 1)
                dve.wait_ge(S["zb_done"], l * 2 + 2)
                V.scalar_tensor_tensor(out=ex[:, 0:2, :], in0=bcum[:, :, :], scalar=-1.0, in1=bcum[:, :, :],
                                       op0=ALU.mult, op1=ALU.max).then_inc(S["abs_done"], 1)
                dve.wait_ge(S["ln_done"], l + 1)
                step("b_step", 2, V.scalar_tensor_tensor(out=bcum[:, :, :], in0=bcum[:, :, :], scalar=0.0,
                                                         in1=ex[:, 0:2, :], op0=ALU.min, op1=ALU.subtract))
                step("b_step", 2, V.tensor_tensor_scan(bcum[:, 0, :], chunk_mask[:, :], bcum[:, 0, :], 0.0,
                                                       ALU.mult, ALU.add))
                V.tensor_tensor_scan(bcum[:, 1, :], chunk_mask[:, :], bcum[:, 1, :], 0.0,
                                     ALU.mult, ALU.add).then_inc(S["b_done"], 1)
                dve.wait_ge(S["b_done"], l + 1)

                def chunks(ap, n=CH, upto=SEQ):
                    return ap[:, :, 0:upto].rearrange("p t (c i) -> p t c i", i=n)

                b4 = chunks(bcum)
                for t in range(2):
                    i = V.tensor_tensor(chunks(pair_exp[1])[:, t], b4[:, t, :, CH - 1:CH].to_broadcast([P, NCH, CH]),
                                        b4[:, t], ALU.subtract)
                    i.then_inc(S["arg_done"] if t == 1 else S["arg_step"], 1)
                dve.wait_ge(S["exp_done"], l * 9 + 1)
                V.tensor_copy(elast[:, :, :], chunks(pair_exp[0])[:, :, :, CH - 1])
                V.tensor_tensor(qe[:, :, :], qk[:, 0:2, :], pair_exp[0], ALU.mult).then_inc(S["qe_done"], 1)
                dve.wait_ge(S["qe_done"], l + 1)

                def arguments(i):
                    s = LEVELS[i]
                    upto = T if s <= META // 2 else SEQ
                    e = chunks(pair_exp[i % 2], 2 * s, upto)
                    b = chunks(bcum, 2 * s, upto)
                    nb = upto // (2 * s)
                    for t in range(2):
                        ref = b[:, t, :, s - 1:s].to_broadcast([P, nb, s])
                        V.tensor_tensor(e[:, t, :, 0:s], ref, b[:, t, :, 0:s], ALU.subtract).then_inc(S["arg_step"], 1)
                        x = V.tensor_tensor(e[:, t, :, s:2 * s], b[:, t, :, s:2 * s], ref, ALU.subtract)
                        x.then_inc(S["arg_step"] if t == 0 else S["arg_done"], 1)

                def decayed(i):
                    s = LEVELS[i]
                    upto = T if s <= META // 2 else SEQ
                    dve.wait_ge(S["exp_done"], l * 9 + (i + 3))
                    if i >= 2:
                        dve.wait_ge(S["lev_acc"], l * 7 + (i - 1))
                    e = pair_exp[i % 2]
                    V.tensor_tensor(kt[:, i % 2, :, 0:upto], qk[:, 2:4, 0:upto], e[:, :, 0:upto],
                                    ALU.mult).then_inc(S["ktqt_step"], 1)
                    e = chunks(e, 2 * s, upto)
                    q = chunks(qk[:, 0:2, :], 2 * s, upto)
                    o = qt[:, i % 2, :, 0:upto // 2].rearrange("p t (c i) -> p t c i", i=s)
                    V.tensor_tensor(o, q[:, :, :, s:2 * s], e[:, :, :, s:2 * s], ALU.mult).then_inc(S["ktqt_done"], 1)
                    dve.wait_ge(S["ktqt_done"], l * 7 + (i + 1))

                def take_level(i):
                    s = LEVELS[i]
                    nb = CH // 2 // s
                    dve.wait_ge(S["masks"], 1)
                    dve.wait_ge(S["lev_acc"], l * 7 + (i + 1))
                    for hp in range(2):
                        dst = acc_a[:, 2 * hp:2 * hp + 2, :, :].rearrange("p h c (b i) -> p (h c) b i", i=2 * s)[:, :, :, s:2 * s]
                        src = PS[2][:, hp, :].rearrange("p (g b i) -> p g b i", b=nb, i=s)
                        msk = level_mask[:, i, :].rearrange("p (o b i) -> p o b i", o=1, i=s).to_broadcast([P, 8, nb, s])
                        x = V.copy_predicated(dst, msk, src)
                        if hp == 0:
                            x.then_inc(S["arg_step"], 1)
                    if s <= META // 2:
                        x.then_inc(S["arg_step"], 1)
                        nb = META // 2 // s
                        dst = acc_t[:, :, :].rearrange("p h (b i) -> p h b i", i=2 * s)[:, :, :, s:2 * s]
                        src = PS[3][0:META, 0, 0:32].rearrange("p (g b i) -> p g b i", b=nb, i=s)
                        msk = level_mask[0:META, i, 0:META // 2].rearrange("p (o b i) -> p o b i", o=1, i=s)\
                            .to_broadcast([META, HEADS, nb, s])
                        x = V.copy_predicated(dst, msk, src)
                    x.then_inc(S["lev_evac"], 1)
                    dve.wait_ge(S["lev_evac"], l * 7 + (i + 1))

                def v_tail_copy(h):
                    dve.wait_ge(S["vtr_acc"], l * 4 + (h + 1))
                    V.tensor_copy(v_tail[:, h, :], PS[3][0:META, 0, 256:256 + DV]).then_inc(S["v_tail_done"], 1)

                def pool_windows(g, idx):
                    u = ft[:, g % 2, :]
                    wait_stream(dve, l, idx)
                    if g < 2:
                        dve.wait_ge(S["vtr_acc"], l * 4 + (g + 3))
                    V.tensor_copy(halves(u), pair(idx % 2)).then_inc(S["u_evac"], 1)
                    dve.wait_ge(S["u_evac"], l * 4 + (g + 1))
                    src = u
                    for j in range(g + 1):
                        sh = 1 << j
                        dst = win[:, j % 2, :]
                        V.tensor_copy(dst[:, 0:sh], src[:, 0:sh]).then_inc(S["arg_step"], 1)
                        step("pool_step", 14, V.tensor_tensor(dst[:, sh:T], src[:, sh:T], src[:, 0:T - sh], ALU.add))
                        src = dst
                    w = WINDOWS[g]
                    step("pool_step", 14, V.tensor_tensor(src[:, 0:w], src[:, 0:w], inv_count[:, 0:w], ALU.mult))
                    V.tensor_tensor(u[:, 0:w], src[:, 0:w], u[:, 0:w], ALU.subtract).then_inc(S["arg_step"], 1)
                    V.scalar_tensor_tensor(out=u[:, w:T], in0=src[:, w:T], scalar=1.0 / w, in1=u[:, w:T],
                                           op0=ALU.mult, op1=ALU.subtract).then_inc(S["pool_done"], 1)
                    dve.wait_ge(S["pool_done"], l * 4 + (g + 1))

                def pool_out(g, idx):
                    wait_stream(dve, l, idx)
                    ps_scale = par[:, C_PS + g:C_PS + g + 1]
                    V.tensor_scalar(halves(yp_hi[:, g, :]), pair(idx % 2), ps_scale, None, ALU.mult).then_inc(S["wsplit_step"], 1)
                    V.tensor_scalar(halves(win[:, 0, :]), pair(idx % 2), ps_scale, None, ALU.mult).then_inc(S["wsplit_step"], 1)
                    dve.wait_ge(S["wsplit_step"], l * 8 + (2 * g + 2))
                    V.tensor_tensor(yp_lo[:, g, :], win[:, 0, :], yp_hi[:, g, :].bitcast(F32),
                                    ALU.subtract).then_inc(S["w_evac"], 1)
                    dve.wait_ge(S["masks"], 1)
                    dve.wait_ge(S["w_evac"], l * 4 + (g + 1))

                def states(t):
                    dve.wait_ge(S["u_acc"], l * 2 + (t + 1))
                    step("s_step", 6, V.tensor_copy(state[:, t, 0, :], PS[3][:, 1, 0:DV]))
                    for c in range(1, NCH):
                        x = V.scalar_tensor_tensor(out=state[:, t, c, :], in0=state[:, t, c - 1, :],
                                                   scalar=elast[:, t, c:c + 1], in1=PS[3][:, 1, c * DV:(c + 1) * DV],
                                                   op0=ALU.mult, op1=ALU.add)
                        if c < NCH - 1:
                            step("s_step", 6, x)
                    x.then_inc(S["s_done"], 1)

                def take_o(h):
                    dve.wait_ge(S["o_acc"], l * 4 + (h + 1))
                    V.tensor_copy(qk[:, h, 0:SEQ], PS[2 + h % 2][:, 0, :]).then_inc(S["arg_step"], 1)
                    V.tensor_copy(qk[:, h, TAIL:T], PS[2 + h % 2][:, 1, 0:META]).then_inc(S["o_done"], 1)

                def finish_o(h):
                    dve.wait_ge(S["rms_std"], l * 4 + (h + 1))
                    step("o_step", 8, V.reciprocal(ex[:, h, :], ex[:, h, :]))
                    step("o_step", 8, V.tensor_tensor(qk[:, h, :], qk[:, h, :], ex[:, h, :], ALU.mult))
                    V.scalar_tensor_tensor(out=qk[:, h, :], in0=qk[:, h, :], scalar=par[:, C_GN + h:C_GN + h + 1],
                                           in1=s_r[:, h, :], op0=ALU.mult, op1=ALU.mult).then_inc(S["o_fin"], 1)

                def split_o(h):
                    dve.wait_ge(S["o_hi_done"], l * 4 + (h + 1))
                    V.tensor_tensor(x_lo[:, h, :], qk[:, h, :], x_hi[:, h, :].bitcast(F32),
                                    ALU.subtract).then_inc(S["o_lo_done"], 1)

                def take_pool_part(mo):
                    idx = 20 + mo
                    wait_stream(dve, l, idx)
                    V.scalar_tensor_tensor(out=halves(X[:, mo, :]), in0=halves(X[:, mo, :]), scalar=ALPHA,
                                           in1=pair(idx % 2), op0=ALU.mult, op1=ALU.add).then_inc(S["wop_evac"], 1)

                arguments(0)
                dve.wait_ge(S["exp_done"], l * 9 + 2)
                V.tensor_tensor(kdec[:, :, :], qk[:, 2:4, 0:SEQ], ex[:, 2:4, 0:SEQ], ALU.mult).then_inc(S["kdec_done"], 1)
                dve.wait_ge(S["kdec_done"], l + 1)
                arguments(1)
                decayed(0)
                arguments(2)
                dve.wait_ge(S["masks"], 1)
                dve.wait_ge(S["diag_acc"], l + 1)
                for hp in range(2):
                    V.copy_predicated(acc_a[:, 2 * hp:2 * hp + 2, :, :].rearrange("p h c i -> p (h c) i"),
                                      ident_mask[:, :].rearrange("p (o i) -> p o i", o=1).to_broadcast([P, 8, P]),
                                      PS[2 + hp][:, :, :].rearrange("p a (c i) -> p (a c) i", i=CH)).then_inc(S["diag_evac"], 1)
                decayed(1)
                arguments(3)
                dve.wait_ge(S["masks"], 1)
                dve.wait_ge(S["tdiag_acc"], l + 1)
                V.copy_predicated(acc_t[:, :, :], ident_mask[0:META, 0:META].rearrange("p (o i) -> p o i", o=1)
                                  .to_broadcast([META, HEADS, META]),
                                  PS[3][0:META, 0, 0:HEADS * META].rearrange("p (h i) -> p h i", i=META))\
                    .then_inc(S["tdiag_evac"], 1)
                v_tail_copy(0)
                take_level(0)
                decayed(2)
                arguments(4)
                v_tail_copy(1)
                take_level(1)
                decayed(3)
                arguments(5)
                v_tail_copy(2)
                take_level(2)
                pool_windows(0, 8)
                v_tail_copy(3)
                decayed(4)
                arguments(6)
                pool_windows(1, 9)
                pool_out(0, 10)
                take_level(3)
                decayed(5)
                pool_windows(2, 11)
                pool_out(1, 12)
                take_level(4)
                decayed(6)
                pool_windows(3, 13)
                pool_out(2, 14)
                take_level(5)
                pool_out(3, 16)
                take_level(6)
                states(0)
                states(1)
                for h in range(HEADS):
                    take_o(h)
                for mo in range(2):
                    take_pool_part(mo)
                finish_o(0)
                take_pool_part(2)
                finish_o(1)
                split_o(0)
                take_pool_part(3)
                finish_o(2)
                split_o(1)
                take_pool_part(4)
                finish_o(3)
                split_o(2)
                take_pool_part(5)
                split_o(3)
                take_pool_part(6)
                take_pool_part(7)
                dve.wait_ge(S["wop_evac"], l * 8 + 8)
                resid(l * LN_PER + 1, lambda mo: stream_ready(l, 28 + mo), 2)

            for ap, val in ((ones_mean[:, :], 1.0 / D), (ones_rms[:, :], 1.0 / DV), (chunk_mask[:, :], 1.0),
                            (ln_eps[:, :], LN_EPS), (rms_eps[:, :], RMS_EPS)):
                i = V.memset(ap, val)
            i.then_inc(S["setup"], 1)
            dve.wait_ge(S["setup"], 1)
            for t in range(META):
                V.memset(inv_count[:, t:t + 1], 1.0 / (t + 1))
            for c in range(1, NCH + 1):
                V.memset(chunk_mask[:, c * CH:c * CH + 1], 0.0)
            V.memset(chunk_mask[:, 0:1], 0.0).then_inc(S["consts_dve"], 1)
            for k in range(KC):
                dve.wait_ge(S["init_hi"], k + 1)
                V.tensor_tensor(x_lo[:, k, :], X[:, k, :], x_hi[:, k, :].bitcast(F32),
                                ALU.subtract).then_inc(S["x_lo_done"], 1)
            dve.wait_ge(S["masks"], 1)
            dve.wait_ge(S["consts_dve"], 1)
            with dve.Fori(0, DEPTH) as l:
                ffn(l, 0)
                norm(l * LN_PER)
                mixer(l)
                norm(l * LN_PER + 1)
                ffn(l, 1)
                norm(l * LN_PER + 2)


def place(h):
    return 2 * (h % 2) + h // 2


def tiles(w):
    k, m = w.shape
    return w.reshape(k // 128, 128, m // 128, 128).transpose(2, 1, 0, 3)


def kernel(x, meta_tokens, ffn1_w_gate, ffn1_w_up, ffn1_w_down, ln1_g, ln1_b, w_in, w_gate_up, b_gate, w_pool,
           pool_scale, gla_norm_g, w_out, ln2_g, ln2_b, ffn2_w_gate, ffn2_w_up, ffn2_w_down, ln3_g, ln3_b):
    import numpy as np
    import concourse.bacc as bacc
    from concourse.bass_utils import run_bass_kernel_spmd

    A = np.asarray
    x_t = np.ascontiguousarray(np.concatenate([A(meta_tokens), A(x)[0]], axis=0).T)
    stream = np.zeros((DEPTH * LAYER_PIECES, P, TILES, P), A(w_in).dtype)
    params = np.zeros((DEPTH + 1, P, C_ALL), A(w_in).dtype)

    n = 0
    for l in range(DEPTH):
        for f, (wg, wu, wd) in enumerate(((ffn1_w_gate, ffn1_w_up, ffn1_w_down), (ffn2_w_gate, ffn2_w_up, ffn2_w_down))):
            g, u, d = (tiles(A(w)[l]) for w in (wg, wu, wd))
            for m0, nm in PHASES:
                for m in range(m0, m0 + nm):
                    stream[n] = g[m]
                    stream[n + 1] = u[m]
                    n += 2
                stream[n:n + KC, :, 0:nm] = d[:, :, m0:m0 + nm]
                n += KC
            if f == 0:
                stream[n:n + MIX_IN] = tiles(A(w_in)[l][:, :16 * P])[list(IN_TILES)]
                n += MIX_IN
                wo = tiles(A(w_out)[l])
                for part in range(2):
                    for mo in range(0, KC, 2):
                        stream[n, :, 0:4] = wo[mo, :, 4 * part:4 * part + 4]
                        stream[n, :, 4:8] = wo[mo + 1, :, 4 * part:4 * part + 4]
                        n += 1
        for r, (g, b) in enumerate(((ln1_g, ln1_b), (ln2_g, ln2_b), (ln3_g, ln3_b))):
            params[l, :, C_LN + 16 * r:C_LN + 16 * r + 8] = A(g)[l].reshape(KC, P).T
            params[l, :, C_LN + 16 * r + 8:C_LN + 16 * r + 16] = A(b)[l].reshape(KC, P).T
        params[l, :, C_BG:C_BG + 2] = A(b_gate)[l].reshape(2, P).T
        params[l, :, C_PS:C_PS + 4] = A(pool_scale)[l].reshape(4, P).T
        params[l, :, C_GN:C_GN + 4] = A(gla_norm_g)[l].reshape(4, P).T
        params[l, :, C_WP:C_GU] = A(w_pool)[l].transpose(1, 0, 2).reshape(P, GROUPS * P)
        params[l, 0:RANK, C_GU:C_GL] = A(w_gate_up)[l]
        params[l, :, C_GL:C_ALL] = A(w_in)[l][:, 16 * P:].reshape(KC, P, RANK).transpose(1, 0, 2).reshape(P, KC * RANK)
    params[DEPTH] = params[DEPTH - 1]
    stream = stream.reshape(DEPTH * LAYER_PIECES // RAWS, RAWS, P, PIECE)

    nc = bacc.Bacc("TRN2", target_bir_lowering=False, num_devices=1)
    arrays = {"in_x_t": x_t, "in_stream": stream, "in_params": params}
    aps = [nc.dram_tensor(name, a.shape, F32, kind="ExternalInput").ap() for name, a in arrays.items()]
    out = nc.dram_tensor("out_t", (D, SEQ), F32, kind="ExternalOutput").ap()
    build(nc, *aps, out)
    r = run_bass_kernel_spmd(nc, [arrays], core_ids=[0])
    return np.ascontiguousarray(r.results[0]["out_t"].T)[None]
```

```python
from contextlib import ExitStack

import concourse.bass as bass
from concourse import mybir

F32 = mybir.dt.float32
F32R = mybir.dt.float32r
I32 = mybir.dt.int32
ALU = mybir.AluOpType
ACT = mybir.ActivationFunctionType

P = 128
D = 1024
SEQ = 512
DEPTH = 2
META = 16
T = SEQ + META
HALF = T // 2
KC = D // P
FF = 2816
MT = FF // P
PHASES = ((0, 8), (8, 8), (16, 6))
POOL_W = 512
GROUPS = 4
KEY_W = 256
HEADS = 4
DK = 64
DV = 128
RANK = 16
GATE_TEMP = 16.0
WINDOWS = (2, 4, 8, 16)
ALPHA = (2.0 * DEPTH) ** 0.25
LN_EPS = 1e-5
RMS_EPS = 1e-6

SLOTS = 4
RAWS = 2
TILES = 8
PIECE = TILES * P

CH = 128
NCH = SEQ // CH
TAIL = NCH * CH
LEVELS = (64, 32, 16, 8, 4, 2, 1)

FFN_PIECES = 2 * MT + len(PHASES) * KC
MIX_IN = 16
MIX_OUT = 8
LAYER_PIECES = 2 * FFN_PIECES + MIX_IN + MIX_OUT
IN_TILES = (4, 5, 6, 7, 8, 9, 10, 11, 0, 1, 2, 3, 12, 13, 14, 15)

C_LN = 0
C_BG = 48
C_PS = 50
C_GN = 54
C_WP = 64
C_GU = C_WP + GROUPS * P
C_GL = C_GU + KEY_W
C_ALL = C_GL + KC * RANK

STREAM = 36
DVE_MIX = 0
GROUPS_ORDER = ([("q", 0), ("q", 1), ("k", 0), ("k", 1)] + [("v", h) for h in range(4)]
                + [("u", 0), ("u", 1), ("w", 0), ("u", 2), ("w", 1), ("u", 3), ("w", 2), ("r", 0), ("w", 3),
                   ("r", 1), ("r", 2), ("r", 3)]
                + [("p", m) for m in range(8)] + [("g", m) for m in range(8)])


def gate_piece(l, f, m):
    phase = max(p for p, (m0, _) in enumerate(PHASES) if m0 <= m)
    return l * LAYER_PIECES + (f * (FFN_PIECES + MIX_IN + MIX_OUT) + 2 * m + KC * phase + 1)


def down_piece(l, f, p, mo):
    return l * LAYER_PIECES + (f * (FFN_PIECES + MIX_IN + MIX_OUT) + 2 * sum(PHASES[p]) + KC * p + mo + 1)


def stream_ready(l, idx):
    kind, n = GROUPS_ORDER[idx]
    if kind == "w":
        return "pw_acc", l * 4 + (n + 1)
    if kind in "pg":
        done = 4 * (kind == "g") + n // 2
        if n % 2 == 0:
            return "out_acc", l * 8 + (done + 1)
        return "piece_done", l * LAYER_PIECES + (FFN_PIECES + MIX_IN + done + 1)
    base = {"q": 0, "k": 2, "v": 4, "u": 8, "r": 12}[kind]
    return "piece_done", l * LAYER_PIECES + (FFN_PIECES + base + n + 1)


def build(nc, x_t, stream, params, out_t):
    ctx = ExitStack()
    with ctx:
        def sb(name, shape, dt=F32, where=ctx):
            return where.enter_context(nc.sbuf_tensor(name, shape, dt))

        def sem(name):
            return ctx.enter_context(nc.semaphore(name))

        raw = sb("raw", [P, RAWS, PIECE])
        w_hi = sb("w_hi", [P, SLOTS, PIECE], F32R)
        w_lo = sb("w_lo", [P, SLOTS, PIECE], F32R)
        X = sb("X", [P, KC, T])
        x_hi = sb("x_hi", [P, KC, T], F32R)
        x_lo = sb("x_lo", [P, KC, T], F32R)
        par = sb("par", [P, C_ALL])
        ones_mean = sb("ones_mean", [P, P])
        ones_rms = sb("ones_rms", [P, P])
        ident = sb("ident", [P, P])
        ident_mask = sb("ident_mask", [P, P], I32)
        level_mask = sb("level_mask", [P, len(LEVELS), CH // 2], I32)
        chunk_mask = sb("chunk_mask", [P, T])
        inv_count = sb("inv_count", [P, META])
        warm = sb("warm", [P, 2])
        rms_eps = sb("rms_eps", [P, 1])
        acc_a = sb("acc_a", [P, HEADS, NCH, CH])
        acc_t = sb("acc_t", [META, HEADS, META])
        with ExitStack() as s1:
            sum_x = sb("sum_x", [P, T], F32, s1)
            sum_sq = sb("sum_sq", [P, T], F32, s1)
            sq = sb("sq", [P, 2, T], F32, s1)
            mean_sq = sb("mean_sq", [P, T], F32, s1)
            var = sb("var", [P, T], F32, s1)
            rstd = sb("rstd", [P, T], F32, s1)
            mean = sb("mean", [P, T], F32, s1)
            xhat = sb("xhat", [P, 2, T], F32, s1)
        with ExitStack() as s2:
            ex = sb("ex", [P, 4, T], F32, s2)
            kt = sb("kt", [P, 2, 2, T], F32, s2)
            qt = sb("qt", [P, 2, 2, HALF], F32, s2)
        sb("reserve_ln", [P, 10 * T])
        with ExitStack() as s3:
            h_hi = sb("h_hi", [P, TILES, T], F32R, s3)
            h_lo = sb("h_lo", [P, TILES, T], F32R, s3)
            silu = sb("silu", [P, T], F32, s3)
            prod = sb("prod", [P, T], F32, s3)
        yp_hi = sb("yp_hi", [P, GROUPS, T], F32R)
        yp_lo = sb("yp_lo", [P, GROUPS, T], F32R)
        qk = sb("qk", [P, 4, T])
        bcum = sb("bcum", [P, 2, T])
        kdec = sb("kdec", [P, 2, SEQ])
        qe = sb("qe", [P, 2, T])
        elast = sb("elast", [P, 2, NCH])
        ft = sb("ft", [P, 2, T])
        win = sb("win", [P, 2, T])
        v_tok = sb("v_tok", [P, HEADS, NCH, DV])
        v_tail = sb("v_tail", [META, HEADS, DV])
        kd_tok = sb("kd_tok", [P, 2, NCH, CH])
        state = sb("state", [P, 2, NCH, DV])
        s_r = sb("s_r", [P, HEADS, T])
        glr = sb("glr", [RANK, T])

        PS = [ctx.enter_context(nc.psum_tensor(f"PS{i}", [P, 2, 512], F32)) for i in range(4)]

        def pair(i):
            return PS[i][:, :, 0:HALF]

        def halves(ap):
            return ap.rearrange("p (a b) -> p a b", a=2)

        names = """par_loaded consts consts_dve masks raw_hi split_done piece_done out_stored setup row_sync
            silu_done prod_done h_hi_done h_lo_done down_evac
            resid_done sq_done s1_done s2_done mean_acc msq_acc mean_sq_done var_done std_done rstd_done mean_done
            centered xhat_done x_hi_done x_full_done x_lo_done warm_done
            pw_acc out_acc qkv_evac u_evac w_evac sr_evac wop_evac glr_acc glr_done z_acc zb_done abs_done en_done
            ln_done b_step b_done arg_step arg_done exp_done qe_done kdec_done ktqt_step ktqt_done lev_acc lev_evac
            diag_acc diag_evac tdiag_acc tdiag_evac vtr_acc v_tok_done v_tail_done ktr_acc kd_tok_done
            u_acc s_step s_done pool_step pool_done wsplit_step o_acc o_done osq_done ms_acc rms_std o_step o_fin
            o_hi_done o_lo_done acc_zero""".split()
        S = {n: sem(n) for n in names}
        x_loaded = [sem(f"x_loaded{k}") for k in range(KC)]
        raw_full = [sem(f"raw_full{i}") for i in range(RAWS)]
        block = ctx.enter_context(nc.Block())

        LN_PER = 3

        def wait_stream(eng, l, idx):
            name, value = stream_ready(l, idx)
            eng.wait_ge(S[name], value)

        @block.sync
        def _(sp):
            for n in range(RAWS):
                sp.dma_start(raw[:, n, :], stream[0, n]).then_inc(raw_full[n], 16)
            with sp.Fori(1, (DEPTH * LAYER_PIECES + SLOTS) // RAWS) as i:
                for n in range(RAWS):
                    sp.wait_ge(S["split_done"], i * RAWS + (n - RAWS + 1))
                    sp.dma_start(raw[:, n, :], stream[i, n]).then_inc(raw_full[n], 16)
            for k in range(KC):
                sp.wait_ge(S["x_full_done"], DEPTH * LN_PER * KC - KC + k + 1)
                sp.dma_start(out_t[k * P:(k + 1) * P, :], X[:, k, META:T]).then_inc(S["out_stored"], 16)
            sp.wait_ge(S["out_stored"], 16 * KC)

        @block.gpsimd
        def _(pool):
            def split(slot, done):
                pool.wait_ge(S["raw_hi"], done)
                nc.gpsimd.tensor_tensor(w_lo[:, slot, :], raw[:, slot % RAWS, :], w_hi[:, slot, :].bitcast(F32),
                                        ALU.subtract).then_inc(S["split_done"], 1)

            for n in range(SLOTS):
                split(n, n + 1)
            nc.gpsimd.memset(level_mask[:, :, :], 1).then_inc(S["consts"], 1)
            nc.gpsimd.memset(ident_mask[:, :], 0).then_inc(S["consts"], 1)
            nc.gpsimd.memset(ident[:, :], 0.0).then_inc(S["consts"], 1)
            pool.wait_ge(S["consts"], 3)
            n = 3
            for m in (ident_mask, ident):
                nc.gpsimd.affine_select(out=m[:, :], in_=m[:, :], compare_op=ALU.not_equal, fill=1.0, base=0,
                                        pattern=[[-1, P]], channel_multiplier=1).then_inc(S["consts"], 1)
            n += 2
            for i, s in enumerate(LEVELS):
                m = level_mask[:, i, :].rearrange("p (b s) -> p b s", s=s)
                nb = CH // 2 // s
                nc.gpsimd.affine_select(out=m, in_=m, compare_op=ALU.is_ge, fill=0.0, base=0,
                                        pattern=[[-2 * s, nb], [0, s]], channel_multiplier=1).then_inc(S["consts"], 1)
                n += 1
                pool.wait_ge(S["consts"], n)
                nc.gpsimd.affine_select(out=m, in_=m, compare_op=ALU.is_ge, fill=0.0, base=s - 1,
                                        pattern=[[2 * s, nb], [0, s]], channel_multiplier=-1).then_inc(S["consts"], 1)
                n += 1
                pool.wait_ge(S["consts"], n)
            nc.gpsimd.memset(acc_t[:, :, :], 0.0).then_inc(S["masks"], 1)
            with pool.Fori(1, DEPTH * LAYER_PIECES // SLOTS + 1) as i:
                for n in range(SLOTS):
                    split(n, i * SLOTS + (n + 1))

        @block.tensor
        def _(pe):
            def tile_products(ps, slot, t, k, rhs_hi, rhs_lo, first, last, half):
                hi = w_hi[:, slot, t * P:(t + 1) * P]
                lo = w_lo[:, slot, t * P:(t + 1) * P]
                tok = slice(half * HALF, (half + 1) * HALF)
                o = PS[ps][:, half, 0:HALF]
                nc.tensor.matmul(o, hi, rhs_hi[:, k, tok], start=first, stop=False)
                nc.tensor.matmul(o, hi, rhs_lo[:, k, tok], start=False, stop=False)
                return nc.tensor.matmul(o, lo, rhs_hi[:, k, tok], start=False, stop=last)

            def chunk_products(LN, k, n):
                pe.wait_ge(S["x_hi_done"], LN * KC + (k + 1))
                hi = [w_hi[:, j, k * P:(k + 1) * P] for j in range(n)]
                lo = [w_lo[:, j, k * P:(k + 1) * P] for j in range(n)]
                for j in range(n):
                    for half in range(2):
                        tok = slice(half * HALF, (half + 1) * HALF)
                        nc.tensor.matmul(PS[j][:, half, 0:HALF], hi[j], x_hi[:, k, tok], start=k == 0, stop=False)
                        nc.tensor.matmul(PS[j][:, half, 0:HALF], lo[j], x_hi[:, k, tok], start=False, stop=False)
                pe.wait_ge(S["x_lo_done"], LN * KC + (k + 1))
                for j in range(n):
                    for half in range(2):
                        tok = slice(half * HALF, (half + 1) * HALF)
                        m = nc.tensor.matmul(PS[j][:, half, 0:HALF], hi[j], x_lo[:, k, tok], start=False,
                                             stop=k == KC - 1)
                    if k == KC - 1:
                        m.then_inc(S["piece_done"], 1)

            def product(ps, slot, rhs_hi, rhs_lo, n, t0=0, k0=0):
                for k in range(n):
                    for half in range(2):
                        m = tile_products(ps, slot, t0 + k, k0 + k, rhs_hi, rhs_lo, k == 0, k == n - 1, half)
                return m

            def ffn(l, f):
                F22, FP, FD = l * 44 + 22 * f, l * LAYER_PIECES + f * (FFN_PIECES + MIX_IN + MIX_OUT), \
                    l * 32 + 16 * f
                LN = l * LN_PER + 2 * f
                piece = 0
                for p, (m0, nm) in enumerate(PHASES):
                    last_phase = p == len(PHASES) - 1
                    prev = 16 * 0

                    def gate_up(i, first, base):
                        for j in range(4):
                            m = i * 2 + (m0 + j // 2)
                            pe.wait_ge(S["split_done"], FP + i * 4 + (base + j + 1))
                            if not first:
                                pe.wait_ge(S["silu_done" if j % 2 == 0 else "prod_done"], F22 + m - 1)
                            elif p > 0:
                                pe.wait_ge(S["down_evac"], FD + (8 * (p - 1) + 4 + j + 1))
                            product(j, j, x_hi, x_lo, KC).then_inc(S["piece_done"], 1)

                    if p == 0:
                        for j in range(3):
                            pe.wait_ge(S["split_done"], FP + (j + 1))
                        for k in range(KC):
                            chunk_products(LN, k, 3)
                        pe.wait_ge(S["split_done"], FP + 4)
                        product(3, 3, x_hi, x_lo, KC).then_inc(S["piece_done"], 1)
                    else:
                        gate_up(0, True, piece)
                    with pe.Fori(1, nm // 2) as i:
                        gate_up(i, False, piece)
                    piece += 2 * nm
                    for mo in range(KC):
                        j = mo % 4
                        pe.wait_ge(S["split_done"], FP + (piece + mo + 1))
                        if mo < 4:
                            pe.wait_ge(S["silu_done" if j % 2 == 0 else "prod_done"],
                                       F22 + (m0 + nm - 1 + mo // 2))
                        elif last_phase:
                            pe.wait_ge(S["resid_done"], LN * KC + (mo - 3))
                        else:
                            pe.wait_ge(S["down_evac"], FD + (8 * p + mo - 3))
                        for k in range(nm):
                            if mo == 0:
                                pe.wait_ge(S["h_lo_done"], F22 + (m0 + k + 1))
                            for half in range(2):
                                m = tile_products(j, (piece + mo) % 4, k, k, h_hi, h_lo, k == 0, k == nm - 1, half)
                        m.then_inc(S["piece_done"], 1)
                    piece += KC

            def ln_stats(LN):
                def sums(ps, parts):
                    for n, part in enumerate(parts):
                        for half in range(2):
                            m = nc.tensor.matmul(PS[ps][:, half, 0:HALF], ones_mean[:, :],
                                                 part[:, half * HALF:(half + 1) * HALF], start=n == 0, stop=n == 1)
                        yield m

                pe.wait_ge(S["s1_done"], LN * 6 + 6)
                mean = sums(0, (sum_x, X[:, KC - 1, :]))
                next(mean)
                pe.wait_ge(S["s2_done"], LN * 6 + 6)
                msq = sums(1, (sum_sq, sq[:, (KC - 1) % 2, :]))
                next(msq)
                pe.wait_ge(S["resid_done"], LN * KC + KC)
                next(mean).then_inc(S["mean_acc"], 1)
                pe.wait_ge(S["sq_done"], LN * KC + KC)
                next(msq).then_inc(S["msq_acc"], 1)

            def group_free(l, idx):
                kind, n = GROUPS_ORDER[idx]
                at = {"q": ("qkv_evac", 8, n), "k": ("qkv_evac", 8, 2 + n), "v": ("qkv_evac", 8, 4 + n),
                      "u": ("u_evac", 4, n), "w": ("w_evac", 4, n), "r": ("sr_evac", 4, n),
                      "p": ("wop_evac", 8, n)}.get(kind)
                if kind == "g":
                    pe.wait_ge(S["resid_done"], l * 24 + (8 + n + 1))
                else:
                    pe.wait_ge(S[at[0]], l * at[1] + (at[2] + 1))

            def mixer(l):
                FP = l * LAYER_PIECES + FFN_PIECES
                LN = l * LN_PER + 1
                for j in range(2):
                    pe.wait_ge(S["split_done"], FP + (j + 1))
                pe.wait_ge(S["par_loaded"], l * 16 + 16)
                for k in range(KC):
                    chunk_products(LN, k, 2)
                    for half in range(2):
                        m = nc.tensor.matmul(PS[2][0:RANK, half, 0:HALF], par[:, C_GL + k * RANK:C_GL + (k + 1) * RANK],
                                             X[:, k, half * HALF:(half + 1) * HALF], start=k == 0, stop=k == KC - 1)
                m.then_inc(S["glr_acc"], 1)
                pieces = [2]

                def project(idx):
                    pe.wait_ge(S["split_done"], FP + (pieces[0] + 1))
                    group_free(l, idx - 2)
                    product(idx % 2, pieces[0] % 4, x_hi, x_lo, KC).then_inc(S["piece_done"], 1)
                    pieces[0] += 1

                def pool_product(idx, g):
                    pe.wait_ge(S["pool_done"], l * 4 + (g + 1))
                    group_free(l, idx - 2)
                    for half in range(2):
                        m = nc.tensor.matmul(PS[idx % 2][:, half, 0:HALF], par[:, C_WP + g * P:C_WP + (g + 1) * P],
                                             ft[:, g % 2, half * HALF:(half + 1) * HALF], start=True, stop=True)
                    m.then_inc(S["pw_acc"], 1)

                def gate_logits():
                    pe.wait_ge(S["glr_done"], l + 1)
                    for t in range(2):
                        for half in range(2):
                            m = nc.tensor.matmul(PS[2 + t][:, half, 0:HALF],
                                                 par[0:RANK, C_GU + t * P:C_GU + (t + 1) * P],
                                                 glr[:, half * HALF:(half + 1) * HALF], start=True, stop=True)
                        m.then_inc(S["z_acc"], 1)

                def rows(h):
                    return slice((h % 2) * DK, (h % 2 + 1) * DK)

                def even_tails(product):
                    product(0)
                    product(2).then_inc(S["row_sync"], 1)

                def odd_tails(product):
                    product(1)
                    return product(3)

                def diagonal():
                    pe.wait_ge(S["qkv_evac"], l * 8 + 4)
                    pe.wait_ge(S["zb_done"], l * 2 + 2)
                    for h in range(HEADS):
                        for c in range(NCH):
                            tok = slice(c * CH, (c + 1) * CH)
                            m = nc.tensor.matmul(PS[2 + h % 2][:, h // 2, tok], qk[rows(h), 2 + h // 2, tok],
                                                 qk[rows(h), h // 2, tok], start=True, stop=True)
                    m.then_inc(S["diag_acc"], 1)

                def tail_diagonal(h):
                    return nc.tensor.matmul(PS[3][0:META, 0, place(h) * META:(place(h) + 1) * META],
                                            qk[rows(h), 2 + h // 2, TAIL:T], qk[rows(h), h // 2, TAIL:T],
                                            start=True, stop=True)

                def v_transpose(h):
                    pe.wait_ge(S["qkv_evac"], l * 8 + (4 + h + 1))
                    if h > 0:
                        pe.wait_ge(S["v_tok_done"], l * 4 + h)
                        pe.wait_ge(S["v_tail_done"], l * 4 + h)
                    for c in range(NCH):
                        nc.tensor.transpose(PS[3][:, 1, c * CH:(c + 1) * CH], ft[:, h % 2, c * CH:(c + 1) * CH], ident[:, :])
                    nc.tensor.transpose(PS[3][0:META, 0, 256:256 + DV], ft[:, h % 2, TAIL:T],
                                        ident[:, :]).then_inc(S["vtr_acc"], 1)

                def k_transpose(t):
                    pe.wait_ge(S["kdec_done"], l + 1)
                    if t == 0:
                        pe.wait_ge(S["v_tok_done"], l * 4 + 4)
                    else:
                        pe.wait_ge(S["kd_tok_done"], l * 2 + 1)
                    for c in range(NCH):
                        m = nc.tensor.transpose(PS[3][:, 1, c * CH:(c + 1) * CH], kdec[:, t, c * CH:(c + 1) * CH], ident[:, :])
                    m.then_inc(S["ktr_acc"], 1)

                def level(i):
                    s = LEVELS[i]
                    if i == 0:
                        pe.wait_ge(S["diag_evac"], l * 2 + 2)
                    else:
                        pe.wait_ge(S["lev_evac"], l * 7 + i)
                    if s <= META // 2:
                        pe.wait_ge(S["v_tail_done"], l * 4 + 4)
                    pe.wait_ge(S["ktqt_done"], l * 7 + (i + 1))
                    tail = s <= META // 2

                    def tail_level(h):
                        return nc.tensor.matmul(PS[3][0:META, 0, place(h) * 8:(place(h) + 1) * 8],
                                                kt[rows(h), i % 2, h // 2, TAIL:T], qt[rows(h), i % 2, h // 2, 256:264],
                                                start=True, stop=True)

                    for h in range(HEADS):
                        if tail and h == 1:
                            even_tails(tail_level)
                        for c in range(NCH):
                            if tail and h == 1 and c == 0:
                                pe.wait_ge(S["row_sync"], l * 5 + (i - 1))
                            m = nc.tensor.matmul(PS[2][:, h % 2, (h // 2) * 256 + c * 64:(h // 2) * 256 + (c + 1) * 64],
                                                 kt[rows(h), i % 2, h // 2, c * CH:(c + 1) * CH],
                                                 qt[rows(h), i % 2, h // 2, c * 64:(c + 1) * 64], start=True, stop=True)
                    if tail:
                        m = odd_tails(tail_level)
                    m.then_inc(S["lev_acc"], 1)

                def chunk_updates(t):
                    pe.wait_ge(S["kd_tok_done"], l * 2 + 2)
                    if t == 1:
                        pe.wait_ge(S["s_done"], l * 2 + 1)
                    pe.wait_ge(S["consts_dve"], 1)
                    for h in (2 * t, 2 * t + 1):
                        for c in range(NCH):
                            m = nc.tensor.matmul(PS[3][rows(h), 1, c * DV:(c + 1) * DV], kd_tok[:, t, c, rows(h)],
                                                 v_tok[:, h, c, :], start=True, stop=True)
                    m.then_inc(S["u_acc"], 1)

                def attend(h):
                    ps = 2 + h % 2
                    if h < 2:
                        pe.wait_ge(S["lev_evac"], l * 7 + 7)
                        pe.wait_ge(S["s_done"], l * 2 + 2)
                    else:
                        pe.wait_ge(S["o_done"], l * 4 + (h - 1))
                    for c in range(NCH):
                        tok = slice(c * CH, (c + 1) * CH)
                        if c > 0:
                            nc.tensor.matmul(PS[ps][:, 0, tok], state[rows(h), h // 2, c - 1, :], qe[rows(h), h // 2, tok],
                                             start=True, stop=False)
                        nc.tensor.matmul(PS[ps][:, 0, tok], v_tok[:, h, c, :], acc_a[:, place(h), c, :], start=c == 0, stop=True)
                    nc.tensor.matmul(PS[ps][:, 1, 0:META], state[rows(h), h // 2, NCH - 1, :], qe[rows(h), h // 2, TAIL:T],
                                     start=True, stop=False)
                    nc.tensor.matmul(PS[ps][:, 1, 0:META], v_tail[:, h, :], acc_t[:, place(h), :], start=False,
                                     stop=True).then_inc(S["o_acc"], 1)

                def rms(h):
                    pe.wait_ge(S["osq_done"], l * 4 + (h + 1))
                    if h < 2:
                        pe.wait_ge(S["o_done"], l * 4 + (h + 3))
                    else:
                        pe.wait_ge(S["rms_std"], l * 4 + (h - 1))
                    for half in range(2):
                        m = nc.tensor.matmul(PS[2 + h % 2][:, half, 0:HALF], ones_rms[:, :],
                                             ex[:, h, half * HALF:(half + 1) * HALF], start=True, stop=True)
                    m.then_inc(S["ms_acc"], 1)

                def out_product(idx, mo, part, rhs_hi, rhs_lo):
                    piece = MIX_IN + part * 4 + mo // 2
                    if mo % 2 == 0:
                        pe.wait_ge(S["split_done"], FP + (piece + 1))
                    group_free(l, idx - 2)
                    m = product(idx % 2, piece % 4, rhs_hi, rhs_lo, 4, 4 * (mo % 2))
                    m.then_inc(S["out_acc" if mo % 2 == 0 else "piece_done"], 1)

                project(2)
                gate_logits()
                project(3)
                project(4)
                diagonal()
                project(5)
                pe.wait_ge(S["masks"], 1)
                pe.wait_ge(S["diag_evac"], l * 2 + 2)
                even_tails(tail_diagonal)
                pe.wait_ge(S["row_sync"], l * 5 + 1)
                v_transpose(0)
                odd_tails(tail_diagonal).then_inc(S["tdiag_acc"], 1)
                project(6)
                level(0)
                v_transpose(1)
                project(7)
                level(1)
                v_transpose(2)
                project(8)
                level(2)
                v_transpose(3)
                project(9)
                pool_product(10, 0)
                level(3)
                k_transpose(0)
                project(11)
                pool_product(12, 1)
                level(4)
                k_transpose(1)
                project(13)
                pool_product(14, 2)
                level(5)
                project(15)
                pool_product(16, 3)
                level(6)
                chunk_updates(0)
                project(17)
                chunk_updates(1)
                project(18)
                attend(0)
                attend(1)
                project(19)
                attend(2)
                attend(3)
                pe.wait_ge(S["w_evac"], l * 4 + 4)
                for mo in range(8):
                    out_product(20 + mo, mo, 0, yp_hi, yp_lo)
                    if mo in (1, 3):
                        rms(mo - 1)
                        rms(mo)
                pe.wait_ge(S["o_lo_done"], l * 4 + 4)
                for mo in range(8):
                    out_product(28 + mo, mo, 1, x_hi, x_lo)

            pe.wait_ge(S["masks"], 1)
            pe.wait_ge(S["consts_dve"], 1)
            with pe.Fori(0, DEPTH) as l:
                ffn(l, 0)
                ln_stats(l * LN_PER)
                mixer(l)
                ln_stats(l * LN_PER + 1)
                ffn(l, 1)
                ln_stats(l * LN_PER + 2)

        @block.scalar
        def _(act):
            def ffn(l, f):
                F22 = l * 44 + 22 * f
                n = f * (FFN_PIECES + MIX_IN + MIX_OUT)
                for m in range(MT):
                    phase = max(p for p, (m0, _) in enumerate(PHASES) if m0 <= m)
                    act.wait_ge(S["piece_done"], gate_piece(l, f, m))
                    nc.scalar.activation(halves(silu[:, :]), pair(2 * (m % 2)), ACT.Silu).then_inc(S["silu_done"], 1)
                    high(l, n + SLOTS)
                    act.wait_ge(S["prod_done"], F22 + (m + 1))
                    nc.scalar.activation(h_hi[:, m - PHASES[phase][0], :], prod[:, :], ACT.Copy).then_inc(S["h_hi_done"], 1)
                    high(l, n + 1 + SLOTS)
                    n += 2
                    if m == sum(PHASES[phase]) - 1 and m < MT - 1:
                        for mo in range(KC):
                            high(l, n + SLOTS)
                            n += 1
                squares(l, 2 * f, n, 1)

            def high(l, n):
                act.wait_ge(S["piece_done"], l * LAYER_PIECES + (n - SLOTS + 1))
                act.wait_ge(raw_full[n % RAWS], l * (16 * LAYER_PIECES // RAWS) + 16 * (n // RAWS + 1))
                nc.scalar.activation(w_hi[:, n % SLOTS, :], raw[:, n % RAWS, :], ACT.Copy).then_inc(S["raw_hi"], 1)

            def squares(l, r, n, per_piece):
                LN = l * LN_PER + r
                nc.scalar.activation(warm[:, 1:2], warm[:, 0:1], ACT.Sqrt).then_inc(S["warm_done"], 1)
                for k in range(KC):
                    act.wait_ge(S["resid_done"], LN * KC + (k + 1))
                    if k >= 2:
                        act.wait_ge(S["s2_done"], LN * 6 + max(k - 2, 1))
                    nc.scalar.activation(sq[:, k % 2, :], X[:, k, :], ACT.Square).then_inc(S["sq_done"], 1)
                    if (k + 1) % per_piece == 0 and k < KC - 1:
                        high(l, n + SLOTS)
                        n += 1

            def norm(l, r, n):
                LN = l * LN_PER + r
                act.wait_ge(S["var_done"], LN + 1)
                nc.scalar.activation(mean_sq[:, :], var[:, :], ACT.Sqrt).then_inc(S["std_done"], 1)
                high(l, n + SLOTS)
                g = C_LN + 16 * r
                for k in range(KC):
                    act.wait_ge(S["xhat_done"], LN * KC + (k + 1))
                    nc.scalar.activation(x_hi[:, k, :], xhat[:, k % 2, :], ACT.Identity, bias=par[:, g + 8 + k:g + 9 + k],
                                         scale=par[:, g + k:g + k + 1]).then_inc(S["x_hi_done"], 1)
                    nc.scalar.activation(X[:, k, :], xhat[:, k % 2, :], ACT.Identity, bias=par[:, g + 8 + k:g + 9 + k],
                                         scale=par[:, g + k:g + k + 1]).then_inc(S["x_full_done"], 1)

            def mixer(l):
                def evac(idx, out, scale=1.0):
                    wait_stream(act, l, idx)
                    nc.scalar.activation(halves(out), pair(idx % 2), ACT.Copy, scale=scale).then_inc(S["qkv_evac"], 1)

                def exp_of(i):
                    act.wait_ge(S["arg_done"], l * 8 + (i + 2))
                    e = ex[:, 2 * (i % 2):2 * (i % 2) + 2, :] if LEVELS[i] <= META // 2 else \
                        ex[:, 2 * (i % 2):2 * (i % 2) + 2, 0:SEQ]
                    nc.scalar.activation(e, e, ACT.Exp, scale=1.0 / GATE_TEMP).then_inc(S["exp_done"], 1)

                def v_to_tokens(h):
                    act.wait_ge(S["vtr_acc"], l * 4 + (h + 1))
                    nc.scalar.activation(v_tok[:, h, :, :].rearrange("p c d -> p (c d)"), PS[3][:, 1, :],
                                         ACT.Copy).then_inc(S["v_tok_done"], 1)

                def k_to_tokens(t):
                    act.wait_ge(S["ktr_acc"], l * 2 + (t + 1))
                    nc.scalar.activation(kd_tok[:, t, :, :].rearrange("p c d -> p (c d)"), PS[3][:, 1, :],
                                         ACT.Copy).then_inc(S["kd_tok_done"], 1)

                n0 = FFN_PIECES + SLOTS
                evac(0, qk[:, 0, :], DK ** -0.5)
                evac(1, qk[:, 1, :], DK ** -0.5)
                high(l, n0)
                high(l, n0 + 1)
                evac(2, qk[:, 2, :])
                high(l, n0 + 2)
                for t in range(2):
                    act.wait_ge(S["z_acc"], l * 2 + (t + 1))
                    nc.scalar.activation(halves(bcum[:, t, :]), pair(2 + t), ACT.Identity,
                                         bias=par[:, C_BG + t:C_BG + t + 1]).then_inc(S["zb_done"], 1)
                act.wait_ge(S["abs_done"], l + 1)
                nc.scalar.activation(ex[:, 0:2, :], ex[:, 0:2, :], ACT.Exp, scale=-1.0).then_inc(S["en_done"], 1)
                act.wait_ge(S["en_done"], l + 1)
                nc.scalar.activation(ex[:, 0:2, :], ex[:, 0:2, :], ACT.Ln, bias=1.0).then_inc(S["ln_done"], 1)
                evac(3, qk[:, 3, :])
                high(l, n0 + 3)
                act.wait_ge(S["b_done"], l + 1)
                nc.scalar.activation(ex[:, 0:2, :], bcum[:, :, :], ACT.Exp, scale=1.0 / GATE_TEMP).then_inc(S["exp_done"], 1)
                act.wait_ge(S["arg_done"], l * 8 + 1)
                nc.scalar.activation(ex[:, 2:4, 0:SEQ], ex[:, 2:4, 0:SEQ], ACT.Exp,
                                     scale=1.0 / GATE_TEMP).then_inc(S["exp_done"], 1)
                evac(4, ft[:, 0, :])
                high(l, n0 + 4)
                exp_of(0)
                evac(5, ft[:, 1, :])
                high(l, n0 + 5)
                exp_of(1)
                v_to_tokens(0)
                exp_of(2)
                evac(6, ft[:, 0, :])
                high(l, n0 + 6)
                v_to_tokens(1)
                exp_of(3)
                evac(7, ft[:, 1, :])
                high(l, n0 + 7)
                v_to_tokens(2)
                exp_of(4)
                high(l, n0 + 8)
                v_to_tokens(3)
                exp_of(5)
                high(l, n0 + 9)
                k_to_tokens(0)
                exp_of(6)
                high(l, n0 + 10)
                k_to_tokens(1)
                high(l, n0 + 11)
                for h, idx in enumerate((15, 17, 18, 19)):
                    wait_stream(act, l, idx)
                    nc.scalar.activation(halves(s_r[:, h, :]), pair(idx % 2), ACT.Silu).then_inc(S["sr_evac"], 1)
                    high(l, n0 + 12 + h)
                for h in range(HEADS):
                    act.wait_ge(S["o_done"], l * 4 + (h + 1))
                    nc.scalar.activation(ex[:, h, :], qk[:, h, :], ACT.Square).then_inc(S["osq_done"], 1)

                def rms_std(h):
                    act.wait_ge(S["ms_acc"], l * 4 + (h + 1))
                    nc.scalar.activation(halves(ex[:, h, :]), pair(2 + h % 2), ACT.Sqrt,
                                         bias=rms_eps[:, :]).then_inc(S["rms_std"], 1)

                def o_high(h):
                    act.wait_ge(S["o_fin"], l * 4 + (h + 1))
                    nc.scalar.activation(x_hi[:, h, :], qk[:, h, :], ACT.Copy).then_inc(S["o_hi_done"], 1)

                high(l, n0 + 16)
                rms_std(0)
                rms_std(1)
                o_high(0)
                high(l, n0 + 17)
                rms_std(2)
                rms_std(3)
                o_high(1)
                o_high(2)
                high(l, n0 + 18)
                o_high(3)
                high(l, n0 + 19)
                squares(l, 1, FFN_PIECES + 20, 2)

            for k in range(KC):
                act.dma_start(X[:, k, :], x_t[k * P:(k + 1) * P, :]).then_inc(x_loaded[k], 16)
            act.dma_start(par[:, :], params[0]).then_inc(S["par_loaded"], 16)
            for n in range(SLOTS):
                act.wait_ge(raw_full[n % RAWS], 16 * (n // RAWS + 1))
                nc.scalar.activation(w_hi[:, n, :], raw[:, n % RAWS, :], ACT.Copy).then_inc(S["raw_hi"], 1)
                for k in ((0, 1, 2), (3, 4), (5, 6), (7,))[n]:
                    act.wait_ge(x_loaded[k], 16)
                    nc.scalar.activation(x_hi[:, k, :], X[:, k, :], ACT.Copy).then_inc(S["x_hi_done"], 1)
            act.wait_ge(S["consts_dve"], 1)
            act.wait_ge(S["par_loaded"], 16)
            with act.Fori(0, DEPTH) as l:
                ffn(l, 0)
                norm(l, 0, FFN_PIECES - 1)
                mixer(l)
                norm(l, 1, FFN_PIECES + MIX_IN + MIX_OUT - 1)
                ffn(l, 1)
                norm(l, 2, LAYER_PIECES - 1)
                act.wait_ge(S["x_full_done"], l * 24 + 24)
                act.dma_start(par[:, :], params[l + 1]).then_inc(S["par_loaded"], 16)
                act.wait_ge(S["par_loaded"], l * 16 + 32)

        @block.vector
        def _(dve):
            V = nc.vector

            def ffn(l, f):
                F22 = l * 44 + 22 * f
                down = 0
                FD = l * 48 + 24 * f
                for p, (m0, nm) in enumerate(PHASES):
                    for m in range(m0, m0 + nm):
                        dve.wait_ge(S["silu_done"], F22 + (m + 1))
                        dve.wait_ge(S["piece_done"], gate_piece(l, f, m) + 1)
                        if m > 0:
                            dve.wait_ge(S["h_lo_done"], F22 + m)
                        V.scalar_tensor_tensor(out=halves(prod[:, :]), in0=pair(2 * (m % 2) + 1), scalar=0.5,
                                               in1=halves(silu[:, :]), op0=ALU.mult, op1=ALU.mult).then_inc(S["prod_done"], 1)
                        dve.wait_ge(S["h_hi_done"], F22 + (m + 1))
                        V.tensor_tensor(h_lo[:, m - m0, :], prod[:, :], h_hi[:, m - m0, :].bitcast(F32),
                                        ALU.subtract).then_inc(S["h_lo_done"], 1)
                    if p == len(PHASES) - 1:
                        resid(l * LN_PER + 2 * f, lambda mo: ("piece_done", down_piece(l, f, p, mo)), 4)
                        break
                    for mo in range(KC):
                        dve.wait_ge(S["piece_done"], down_piece(l, f, p, mo))
                        if p == 0:
                            V.scalar_tensor_tensor(out=halves(X[:, mo, :]), in0=halves(X[:, mo, :]), scalar=ALPHA,
                                                   in1=pair(mo % 4), op0=ALU.mult, op1=ALU.add).then_inc(S["down_evac"], 1)
                        else:
                            dve.wait_ge(S["down_evac"], l * 32 + 16 * f + 8)
                            V.tensor_tensor(halves(X[:, mo, :]), halves(X[:, mo, :]), pair(mo % 4),
                                            ALU.add).then_inc(S["down_evac"], 1)

            def resid(LN, ready, pairs):
                def add_square(k):
                    dve.wait_ge(S["sq_done"], LN * KC + (k + 1))
                    if k == 1:
                        V.tensor_tensor(sum_sq[:, :], sq[:, 0, :], sq[:, 1, :], ALU.add).then_inc(S["s2_done"], 1)
                    elif k > 1:
                        dve.wait_ge(S["s2_done"], LN * 6 + (k - 1))
                        V.tensor_tensor(sum_sq[:, :], sum_sq[:, :], sq[:, k % 2, :], ALU.add).then_inc(S["s2_done"], 1)

                for mo in range(KC):
                    name, value = ready(mo)
                    dve.wait_ge(S[name], value)
                    V.tensor_tensor(halves(X[:, mo, :]), halves(X[:, mo, :]), pair(mo % pairs),
                                    ALU.add).then_inc(S["resid_done"], 1)
                    if mo >= 1:
                        add_square(mo - 1)
                    if 1 <= mo < KC - 1:
                        dve.wait_ge(S["resid_done"], LN * KC + (mo + 1))
                        if mo > 1:
                            dve.wait_ge(S["s1_done"], LN * 6 + (mo - 1))
                        V.tensor_tensor(sum_x[:, :], X[:, 0, :] if mo == 1 else sum_x[:, :], X[:, mo, :],
                                        ALU.add).then_inc(S["s1_done"], 1)

            def norm(LN):
                dve.wait_ge(S["mean_acc"], LN + 1)
                V.tensor_copy(halves(mean[:, :]), pair(0)).then_inc(S["mean_done"], 1)
                dve.wait_ge(S["mean_done"], LN + 1)
                V.tensor_tensor(mean_sq[:, :], mean[:, :], mean[:, :], ALU.mult).then_inc(S["mean_sq_done"], 1)
                dve.wait_ge(S["mean_sq_done"], LN + 1)
                dve.wait_ge(S["msq_acc"], LN + 1)
                V.scalar_tensor_tensor(out=halves(var[:, :]), in0=pair(1), scalar=LN_EPS, in1=halves(mean_sq[:, :]),
                                       op0=ALU.add, op1=ALU.subtract).then_inc(S["var_done"], 1)

                def center(k):
                    V.tensor_tensor(xhat[:, k % 2, :], X[:, k, :], mean[:, :], ALU.subtract).then_inc(S["centered"], 1)

                def lo(k):
                    dve.wait_ge(S["x_full_done"], LN * KC + (k + 1))
                    V.tensor_tensor(x_lo[:, k, :], X[:, k, :], x_hi[:, k, :].bitcast(F32),
                                    ALU.subtract).then_inc(S["x_lo_done"], 1)

                center(0)
                center(1)
                dve.wait_ge(S["std_done"], LN + 1)
                V.reciprocal(rstd[:, :], mean_sq[:, :]).then_inc(S["rstd_done"], 1)
                dve.wait_ge(S["rstd_done"], LN + 1)
                for k in range(KC):
                    dve.wait_ge(S["centered"], LN * KC + (k + 1))
                    V.tensor_tensor(xhat[:, k % 2, :], xhat[:, k % 2, :], rstd[:, :], ALU.mult).then_inc(S["xhat_done"], 1)
                    if k >= 1:
                        lo(k - 1)
                        if k < KC - 1:
                            center(k + 1)
                lo(KC - 1)

            def mixer(l):
                pair_exp = [ex[:, 0:2, :], ex[:, 2:4, :]]
                steps = {"pool": 0, "kq": 0, "arg": 0}

                def step(name, total, ins):
                    steps[name] = steps.get(name, 0) + 1
                    ins.then_inc(S[name], 1)
                    dve.wait_ge(S[name], l * total + steps[name])

                dve.wait_ge(S["glr_acc"], l + 1)
                V.tensor_copy(halves(glr[:, :]), PS[2][0:RANK, :, 0:HALF]).then_inc(S["glr_done"], 1)
                V.memset(acc_a[:, :, :, :], 0.0).then_inc(S["acc_zero"], 1)
                dve.wait_ge(S["zb_done"], l * 2 + 2)
                V.scalar_tensor_tensor(out=ex[:, 0:2, :], in0=bcum[:, :, :], scalar=-1.0, in1=bcum[:, :, :],
                                       op0=ALU.mult, op1=ALU.max).then_inc(S["abs_done"], 1)
                dve.wait_ge(S["ln_done"], l + 1)
                step("b_step", 2, V.scalar_tensor_tensor(out=bcum[:, :, :], in0=bcum[:, :, :], scalar=0.0,
                                                         in1=ex[:, 0:2, :], op0=ALU.min, op1=ALU.subtract))
                step("b_step", 2, V.tensor_tensor_scan(bcum[:, 0, :], chunk_mask[:, :], bcum[:, 0, :], 0.0,
                                                       ALU.mult, ALU.add))
                V.tensor_tensor_scan(bcum[:, 1, :], chunk_mask[:, :], bcum[:, 1, :], 0.0,
                                     ALU.mult, ALU.add).then_inc(S["b_done"], 1)
                dve.wait_ge(S["b_done"], l + 1)

                def chunks(ap, n=CH, upto=SEQ):
                    return ap[:, :, 0:upto].rearrange("p t (c i) -> p t c i", i=n)

                b4 = chunks(bcum)
                for t in range(2):
                    i = V.tensor_tensor(chunks(pair_exp[1])[:, t], b4[:, t, :, CH - 1:CH].to_broadcast([P, NCH, CH]),
                                        b4[:, t], ALU.subtract)
                    i.then_inc(S["arg_done"] if t == 1 else S["arg_step"], 1)
                dve.wait_ge(S["exp_done"], l * 9 + 1)
                V.tensor_copy(elast[:, :, :], chunks(pair_exp[0])[:, :, :, CH - 1])
                V.tensor_tensor(qe[:, :, :], qk[:, 0:2, :], pair_exp[0], ALU.mult).then_inc(S["qe_done"], 1)
                dve.wait_ge(S["qe_done"], l + 1)

                def arguments(i):
                    s = LEVELS[i]
                    upto = T if s <= META // 2 else SEQ
                    e = chunks(pair_exp[i % 2], 2 * s, upto)
                    b = chunks(bcum, 2 * s, upto)
                    nb = upto // (2 * s)
                    for t in range(2):
                        ref = b[:, t, :, s - 1:s].to_broadcast([P, nb, s])
                        V.tensor_tensor(e[:, t, :, 0:s], ref, b[:, t, :, 0:s], ALU.subtract).then_inc(S["arg_step"], 1)
                        x = V.tensor_tensor(e[:, t, :, s:2 * s], b[:, t, :, s:2 * s], ref, ALU.subtract)
                        x.then_inc(S["arg_step"] if t == 0 else S["arg_done"], 1)

                def decayed(i):
                    s = LEVELS[i]
                    upto = T if s <= META // 2 else SEQ
                    dve.wait_ge(S["exp_done"], l * 9 + (i + 3))
                    if i >= 2:
                        dve.wait_ge(S["lev_acc"], l * 7 + (i - 1))
                    e = pair_exp[i % 2]
                    V.tensor_tensor(kt[:, i % 2, :, 0:upto], qk[:, 2:4, 0:upto], e[:, :, 0:upto],
                                    ALU.mult).then_inc(S["ktqt_step"], 1)
                    e = chunks(e, 2 * s, upto)
                    q = chunks(qk[:, 0:2, :], 2 * s, upto)
                    o = qt[:, i % 2, :, 0:upto // 2].rearrange("p t (c i) -> p t c i", i=s)
                    V.tensor_tensor(o, q[:, :, :, s:2 * s], e[:, :, :, s:2 * s], ALU.mult).then_inc(S["ktqt_done"], 1)
                    dve.wait_ge(S["ktqt_done"], l * 7 + (i + 1))

                def take_level(i):
                    s = LEVELS[i]
                    nb = CH // 2 // s
                    dve.wait_ge(S["masks"], 1)
                    dve.wait_ge(S["lev_acc"], l * 7 + (i + 1))
                    for hp in range(2):
                        dst = acc_a[:, 2 * hp:2 * hp + 2, :, :].rearrange("p h c (b i) -> p (h c) b i", i=2 * s)[:, :, :, s:2 * s]
                        src = PS[2][:, hp, :].rearrange("p (g b i) -> p g b i", b=nb, i=s)
                        msk = level_mask[:, i, :].rearrange("p (o b i) -> p o b i", o=1, i=s).to_broadcast([P, 8, nb, s])
                        x = V.copy_predicated(dst, msk, src)
                        if hp == 0:
                            x.then_inc(S["arg_step"], 1)
                    if s <= META // 2:
                        x.then_inc(S["arg_step"], 1)
                        nb = META // 2 // s
                        dst = acc_t[:, :, :].rearrange("p h (b i) -> p h b i", i=2 * s)[:, :, :, s:2 * s]
                        src = PS[3][0:META, 0, 0:32].rearrange("p (g b i) -> p g b i", b=nb, i=s)
                        msk = level_mask[0:META, i, 0:META // 2].rearrange("p (o b i) -> p o b i", o=1, i=s)\
                            .to_broadcast([META, HEADS, nb, s])
                        x = V.copy_predicated(dst, msk, src)
                    x.then_inc(S["lev_evac"], 1)
                    dve.wait_ge(S["lev_evac"], l * 7 + (i + 1))

                def v_tail_copy(h):
                    dve.wait_ge(S["vtr_acc"], l * 4 + (h + 1))
                    V.tensor_copy(v_tail[:, h, :], PS[3][0:META, 0, 256:256 + DV]).then_inc(S["v_tail_done"], 1)

                def pool_windows(g, idx):
                    u = ft[:, g % 2, :]
                    wait_stream(dve, l, idx)
                    if g < 2:
                        dve.wait_ge(S["vtr_acc"], l * 4 + (g + 3))
                    V.tensor_copy(halves(u), pair(idx % 2)).then_inc(S["u_evac"], 1)
                    dve.wait_ge(S["u_evac"], l * 4 + (g + 1))
                    src = u
                    for j in range(g + 1):
                        sh = 1 << j
                        dst = win[:, j % 2, :]
                        V.tensor_copy(dst[:, 0:sh], src[:, 0:sh]).then_inc(S["arg_step"], 1)
                        step("pool_step", 14, V.tensor_tensor(dst[:, sh:T], src[:, sh:T], src[:, 0:T - sh], ALU.add))
                        src = dst
                    w = WINDOWS[g]
                    step("pool_step", 14, V.tensor_tensor(src[:, 0:w], src[:, 0:w], inv_count[:, 0:w], ALU.mult))
                    V.tensor_tensor(u[:, 0:w], src[:, 0:w], u[:, 0:w], ALU.subtract).then_inc(S["arg_step"], 1)
                    V.scalar_tensor_tensor(out=u[:, w:T], in0=src[:, w:T], scalar=1.0 / w, in1=u[:, w:T],
                                           op0=ALU.mult, op1=ALU.subtract).then_inc(S["pool_done"], 1)
                    dve.wait_ge(S["pool_done"], l * 4 + (g + 1))

                def pool_out(g, idx):
                    wait_stream(dve, l, idx)
                    ps_scale = par[:, C_PS + g:C_PS + g + 1]
                    V.tensor_scalar(halves(yp_hi[:, g, :]), pair(idx % 2), ps_scale, None, ALU.mult).then_inc(S["wsplit_step"], 1)
                    V.tensor_scalar(halves(win[:, 0, :]), pair(idx % 2), ps_scale, None, ALU.mult).then_inc(S["wsplit_step"], 1)
                    dve.wait_ge(S["wsplit_step"], l * 8 + (2 * g + 2))
                    V.tensor_tensor(yp_lo[:, g, :], win[:, 0, :], yp_hi[:, g, :].bitcast(F32),
                                    ALU.subtract).then_inc(S["w_evac"], 1)
                    dve.wait_ge(S["masks"], 1)
                    dve.wait_ge(S["w_evac"], l * 4 + (g + 1))

                def states(t):
                    dve.wait_ge(S["u_acc"], l * 2 + (t + 1))
                    step("s_step", 6, V.tensor_copy(state[:, t, 0, :], PS[3][:, 1, 0:DV]))
                    for c in range(1, NCH):
                        x = V.scalar_tensor_tensor(out=state[:, t, c, :], in0=state[:, t, c - 1, :],
                                                   scalar=elast[:, t, c:c + 1], in1=PS[3][:, 1, c * DV:(c + 1) * DV],
                                                   op0=ALU.mult, op1=ALU.add)
                        if c < NCH - 1:
                            step("s_step", 6, x)
                    x.then_inc(S["s_done"], 1)

                def take_o(h):
                    dve.wait_ge(S["o_acc"], l * 4 + (h + 1))
                    V.tensor_copy(qk[:, h, 0:SEQ], PS[2 + h % 2][:, 0, :]).then_inc(S["arg_step"], 1)
                    V.tensor_copy(qk[:, h, TAIL:T], PS[2 + h % 2][:, 1, 0:META]).then_inc(S["o_done"], 1)

                def finish_o(h):
                    dve.wait_ge(S["rms_std"], l * 4 + (h + 1))
                    step("o_step", 8, V.reciprocal(ex[:, h, :], ex[:, h, :]))
                    step("o_step", 8, V.tensor_tensor(qk[:, h, :], qk[:, h, :], ex[:, h, :], ALU.mult))
                    V.scalar_tensor_tensor(out=qk[:, h, :], in0=qk[:, h, :], scalar=par[:, C_GN + h:C_GN + h + 1],
                                           in1=s_r[:, h, :], op0=ALU.mult, op1=ALU.mult).then_inc(S["o_fin"], 1)

                def split_o(h):
                    dve.wait_ge(S["o_hi_done"], l * 4 + (h + 1))
                    V.tensor_tensor(x_lo[:, h, :], qk[:, h, :], x_hi[:, h, :].bitcast(F32),
                                    ALU.subtract).then_inc(S["o_lo_done"], 1)

                def take_pool_part(mo):
                    idx = 20 + mo
                    wait_stream(dve, l, idx)
                    V.scalar_tensor_tensor(out=halves(X[:, mo, :]), in0=halves(X[:, mo, :]), scalar=ALPHA,
                                           in1=pair(idx % 2), op0=ALU.mult, op1=ALU.add).then_inc(S["wop_evac"], 1)

                arguments(0)
                dve.wait_ge(S["exp_done"], l * 9 + 2)
                V.tensor_tensor(kdec[:, :, :], qk[:, 2:4, 0:SEQ], ex[:, 2:4, 0:SEQ], ALU.mult).then_inc(S["kdec_done"], 1)
                dve.wait_ge(S["kdec_done"], l + 1)
                arguments(1)
                decayed(0)
                arguments(2)
                dve.wait_ge(S["masks"], 1)
                dve.wait_ge(S["diag_acc"], l + 1)
                for hp in range(2):
                    V.copy_predicated(acc_a[:, 2 * hp:2 * hp + 2, :, :].rearrange("p h c i -> p (h c) i"),
                                      ident_mask[:, :].rearrange("p (o i) -> p o i", o=1).to_broadcast([P, 8, P]),
                                      PS[2 + hp][:, :, :].rearrange("p a (c i) -> p (a c) i", i=CH)).then_inc(S["diag_evac"], 1)
                decayed(1)
                arguments(3)
                dve.wait_ge(S["masks"], 1)
                dve.wait_ge(S["tdiag_acc"], l + 1)
                V.copy_predicated(acc_t[:, :, :], ident_mask[0:META, 0:META].rearrange("p (o i) -> p o i", o=1)
                                  .to_broadcast([META, HEADS, META]),
                                  PS[3][0:META, 0, 0:HEADS * META].rearrange("p (h i) -> p h i", i=META))\
                    .then_inc(S["tdiag_evac"], 1)
                v_tail_copy(0)
                take_level(0)
                decayed(2)
                arguments(4)
                v_tail_copy(1)
                take_level(1)
                decayed(3)
                arguments(5)
                v_tail_copy(2)
                take_level(2)
                pool_windows(0, 8)
                v_tail_copy(3)
                decayed(4)
                arguments(6)
                pool_windows(1, 9)
                pool_out(0, 10)
                take_level(3)
                decayed(5)
                pool_windows(2, 11)
                pool_out(1, 12)
                take_level(4)
                decayed(6)
                pool_windows(3, 13)
                pool_out(2, 14)
                take_level(5)
                pool_out(3, 16)
                take_level(6)
                states(0)
                states(1)
                for h in range(HEADS):
                    take_o(h)
                for mo in range(2):
                    take_pool_part(mo)
                finish_o(0)
                take_pool_part(2)
                finish_o(1)
                split_o(0)
                take_pool_part(3)
                finish_o(2)
                split_o(1)
                take_pool_part(4)
                finish_o(3)
                split_o(2)
                take_pool_part(5)
                split_o(3)
                take_pool_part(6)
                take_pool_part(7)
                dve.wait_ge(S["wop_evac"], l * 8 + 8)
                resid(l * LN_PER + 1, lambda mo: stream_ready(l, 28 + mo), 2)

            for ap, val in ((ones_mean[:, :], 1.0 / D), (ones_rms[:, :], 1.0 / DV), (chunk_mask[:, :], 1.0),
                            (warm[:, :], 1.0), (rms_eps[:, :], RMS_EPS)):
                i = V.memset(ap, val)
            i.then_inc(S["setup"], 1)
            dve.wait_ge(S["setup"], 1)
            for t in range(META):
                V.memset(inv_count[:, t:t + 1], 1.0 / (t + 1))
            for c in range(1, NCH + 1):
                V.memset(chunk_mask[:, c * CH:c * CH + 1], 0.0)
            V.memset(chunk_mask[:, 0:1], 0.0).then_inc(S["consts_dve"], 1)
            for k in range(KC):
                dve.wait_ge(S["x_hi_done"], k + 1)
                V.tensor_tensor(x_lo[:, k, :], X[:, k, :], x_hi[:, k, :].bitcast(F32),
                                ALU.subtract).then_inc(S["x_lo_done"], 1)
            dve.wait_ge(S["masks"], 1)
            dve.wait_ge(S["consts_dve"], 1)
            with dve.Fori(0, DEPTH) as l:
                ffn(l, 0)
                norm(l * LN_PER)
                mixer(l)
                norm(l * LN_PER + 1)
                ffn(l, 1)
                norm(l * LN_PER + 2)


def place(h):
    return 2 * (h % 2) + h // 2


def tiles(w):
    k, m = w.shape
    return w.reshape(k // 128, 128, m // 128, 128).transpose(2, 1, 0, 3)


def kernel(x, meta_tokens, ffn1_w_gate, ffn1_w_up, ffn1_w_down, ln1_g, ln1_b, w_in, w_gate_up, b_gate, w_pool,
           pool_scale, gla_norm_g, w_out, ln2_g, ln2_b, ffn2_w_gate, ffn2_w_up, ffn2_w_down, ln3_g, ln3_b):
    import numpy as np
    import concourse.bacc as bacc
    from concourse.bass_utils import run_bass_kernel_spmd

    A = np.asarray
    x_t = np.ascontiguousarray(np.concatenate([A(meta_tokens), A(x)[0]], axis=0).T)
    stream = np.zeros((DEPTH * LAYER_PIECES + SLOTS, P, TILES, P), A(w_in).dtype)
    params = np.zeros((DEPTH + 1, P, C_ALL), A(w_in).dtype)

    n = 0
    for l in range(DEPTH):
        for f, (wg, wu, wd) in enumerate(((ffn1_w_gate, ffn1_w_up, ffn1_w_down), (ffn2_w_gate, ffn2_w_up, ffn2_w_down))):
            g, u, d = (tiles(A(w)[l]) for w in (wg, wu, wd))
            for m0, nm in PHASES:
                for m in range(m0, m0 + nm):
                    stream[n] = g[m]
                    stream[n + 1] = u[m]
                    n += 2
                stream[n:n + KC, :, 0:nm] = d[:, :, m0:m0 + nm]
                n += KC
            if f == 0:
                stream[n:n + MIX_IN] = tiles(A(w_in)[l][:, :16 * P])[list(IN_TILES)]
                n += MIX_IN
                wo = tiles(A(w_out)[l])
                for part in range(2):
                    for mo in range(0, KC, 2):
                        stream[n, :, 0:4] = wo[mo, :, 4 * part:4 * part + 4]
                        stream[n, :, 4:8] = wo[mo + 1, :, 4 * part:4 * part + 4]
                        n += 1
        for r, (g, b) in enumerate(((ln1_g, ln1_b), (ln2_g, ln2_b), (ln3_g, ln3_b))):
            params[l, :, C_LN + 16 * r:C_LN + 16 * r + 8] = A(g)[l].reshape(KC, P).T
            params[l, :, C_LN + 16 * r + 8:C_LN + 16 * r + 16] = A(b)[l].reshape(KC, P).T
        params[l, :, C_BG:C_BG + 2] = A(b_gate)[l].reshape(2, P).T
        params[l, :, C_PS:C_PS + 4] = A(pool_scale)[l].reshape(4, P).T
        params[l, :, C_GN:C_GN + 4] = A(gla_norm_g)[l].reshape(4, P).T
        params[l, :, C_WP:C_GU] = A(w_pool)[l].transpose(1, 0, 2).reshape(P, GROUPS * P)
        params[l, 0:RANK, C_GU:C_GL] = A(w_gate_up)[l]
        params[l, :, C_GL:C_ALL] = A(w_in)[l][:, 16 * P:].reshape(KC, P, RANK).transpose(1, 0, 2).reshape(P, KC * RANK)
    params[DEPTH] = params[DEPTH - 1]
    stream = stream.reshape((DEPTH * LAYER_PIECES + SLOTS) // RAWS, RAWS, P, PIECE)

    nc = bacc.Bacc("TRN2", target_bir_lowering=False, num_devices=1)
    arrays = {"in_x_t": x_t, "in_stream": stream, "in_params": params}
    aps = [nc.dram_tensor(name, a.shape, F32, kind="ExternalInput").ap() for name, a in arrays.items()]
    out = nc.dram_tensor("out_t", (D, SEQ), F32, kind="ExternalOutput").ap()
    build(nc, *aps, out)
    r = run_bass_kernel_spmd(nc, [arrays], core_ids=[0])
    return np.ascontiguousarray(r.results[0]["out_t"].T)[None]
```

```python
from contextlib import ExitStack

import concourse.bass as bass
from concourse import mybir

F32 = mybir.dt.float32
F32R = mybir.dt.float32r
I32 = mybir.dt.int32
ALU = mybir.AluOpType
ACT = mybir.ActivationFunctionType

P = 128
D = 1024
SEQ = 512
DEPTH = 2
META = 16
T = SEQ + META
HALF = T // 2
KC = D // P
FF = 2816
MT = FF // P
PHASES = ((0, 8), (8, 8), (16, 6))
GROUPS = 4
KEY_W = 256
HEADS = 4
DK = 64
DV = 128
RANK = 16
GATE_TEMP = 16.0
WINDOWS = (2, 4, 8, 16)
ALPHA = (2.0 * DEPTH) ** 0.25
DVE_CENTERS = 4
QUARTERS = 4
RMS_ROWS = HEADS * QUARTERS
LN_EPS = 1e-5
RMS_EPS = 1e-6

SLOTS = 4
RAWS = 2
TILES = 8
PIECE = TILES * P

CH = 128
NCH = SEQ // CH
TAIL = NCH * CH
LEVELS = (64, 32, 16, 8, 4, 2, 1)

FFN_PIECES = 2 * MT + len(PHASES) * KC
MIX_IN = 16
MIX_OUT = 8
LAYER_PIECES = 2 * FFN_PIECES + MIX_IN + MIX_OUT
IN_TILES = (4, 5, 6, 7, 8, 9, 10, 11, 0, 1, 2, 3, 12, 13, 14, 15)

C_LN = 0
C_BG = 48
C_PS = 50
C_GN = 54
C_WP = 64
C_GU = C_WP + GROUPS * P
C_GL = C_GU + KEY_W
C_ALL = C_GL + KC * RANK

GROUPS_ORDER = ([("q", 0), ("q", 1), ("k", 0), ("k", 1)] + [("v", h) for h in range(4)]
                + [("u", 0), ("u", 1), ("w", 0), ("u", 2), ("w", 1), ("u", 3), ("w", 2), ("r", 0), ("w", 3),
                   ("r", 1), ("r", 2), ("r", 3)]
                + [("p", m) for m in range(8)] + [("g", m) for m in range(8)])


def gate_piece(l, f, m):
    phase = max(p for p, (m0, _) in enumerate(PHASES) if m0 <= m)
    return l * LAYER_PIECES + (f * (FFN_PIECES + MIX_IN + MIX_OUT) + 2 * m + KC * phase + 1)


def down_piece(l, f, p, mo):
    return l * LAYER_PIECES + (f * (FFN_PIECES + MIX_IN + MIX_OUT) + 2 * sum(PHASES[p]) + KC * p + mo + 1)


def stream_ready(l, idx):
    kind, n = GROUPS_ORDER[idx]
    if kind == "w":
        return "pw_acc", l * 4 + (n + 1)
    if kind in "pg":
        done = 4 * (kind == "g") + n // 2
        if n % 2 == 0:
            return "out_acc", l * 8 + (done + 1)
        return "piece_done", l * LAYER_PIECES + (FFN_PIECES + MIX_IN + done + 1)
    base = {"q": 0, "k": 2, "v": 4, "u": 8, "r": 12}[kind]
    return "piece_done", l * LAYER_PIECES + (FFN_PIECES + base + n + 1)


START_ORDER = (("piece", 0), ("x", 0), ("piece", 1), ("piece", 2), ("x", 1), ("x", 2), ("piece", 3),
               ("x", 3), ("x", 4), ("x", 5), ("x", 6), ("x", 7))
START_LOW_ORDER = (("piece", 0), ("piece", 1), ("piece", 2), ("x", 0), ("x", 1), ("x", 2), ("piece", 3),
                   ("x", 3), ("x", 4), ("x", 5), ("x", 6), ("x", 7))

ALL = (0, HALF, 2)
OWN = (META, SEQ, 1)


def halved(span):
    return (span[0], (T - span[0]) // 2, 2)


def stat_blocks(span):
    return (T // 6, 6) if span == ALL else (SEQ // 4, 4)


def build(nc, x_t, stream, params, out_t):
    ctx = ExitStack()
    with ctx:
        def sb(name, shape, dt=F32, where=ctx):
            return where.enter_context(nc.sbuf_tensor(name, shape, dt))

        def sem(name):
            return ctx.enter_context(nc.semaphore(name))

        raw = sb("raw", [P, RAWS, PIECE])
        w_hi = sb("w_hi", [P, SLOTS, PIECE], F32R)
        w_lo = sb("w_lo", [P, SLOTS, PIECE], F32R)
        X = sb("X", [P, KC, T])
        x_hi = sb("x_hi", [P, KC, T], F32R)
        x_lo = sb("x_lo", [P, KC, T], F32R)
        par = sb("par", [P, C_ALL])
        ones_mean = sb("ones_mean", [P, P])
        ones = sb("ones", [P, P])
        w_rank = sb("w_rank", [P, KC, 2 * RANK], F32R)
        col_mean = sb("col_mean", [P, 6])
        col_mean_sq = sb("col_mean_sq", [P, 6])
        col_var = sb("col_var", [P, 6])
        col_std = sb("col_std", [P, 6])
        col_rstd = sb("col_rstd", [P, 6])
        rms_comb = sb("rms_comb", [P, 2 * RMS_ROWS - 1])
        rms_rows = sb("rms_rows", [RMS_ROWS, T // QUARTERS])
        ident = sb("ident", [P, P])
        ident_mask = sb("ident_mask", [P, P], I32)
        level_mask = sb("level_mask", [P, len(LEVELS), CH // 2], I32)
        chunk_mask = sb("chunk_mask", [P, T])
        inv_count = sb("inv_count", [P, META])
        warm = sb("warm", [P, 2])
        rms_eps = sb("rms_eps", [P, 1])
        acc_a = sb("acc_a", [P, HEADS, NCH, CH])
        acc_t = sb("acc_t", [META, HEADS, META])
        with ExitStack() as s1:
            sum_x = sb("sum_x", [P, T], F32, s1)
            sum_sq = sb("sum_sq", [P, T], F32, s1)
            sq = sb("sq", [P, 2, T], F32, s1)
            mean = sb("mean", [P, T], F32, s1)
            xhat = sb("xhat", [P, 2, T], F32, s1)
            diag = sb("diag", [P, T], F32, s1)
        with ExitStack() as s0:
            raw_first = sb("raw_first", [P, SLOTS, PIECE], F32, s0)
        with ExitStack() as s2:
            ex = sb("ex", [P, 4, T], F32, s2)
            kt = sb("kt", [P, 2, 2, T], F32, s2)
            qt = sb("qt", [P, 2, 2, HALF], F32, s2)
        sb("reserve_ln", [P, 10 * T])
        with ExitStack() as s3:
            h_hi = sb("h_hi", [P, TILES, T], F32R, s3)
            h_lo = sb("h_lo", [P, TILES, T], F32R, s3)
            silu = sb("silu", [P, T], F32, s3)
            prod = sb("prod", [P, T], F32, s3)
        yp_hi = sb("yp_hi", [P, GROUPS, T], F32R)
        yp_lo = sb("yp_lo", [P, GROUPS, T], F32R)
        qk = sb("qk", [P, 4, T])
        bcum = sb("bcum", [P, 2, T])
        kdec = sb("kdec", [P, 2, SEQ])
        qe = sb("qe", [P, 2, T])
        elast = sb("elast", [P, 2, NCH])
        ft = sb("ft", [P, 2, T])
        win = sb("win", [P, 2, T])
        v_tok = sb("v_tok", [P, HEADS, NCH, DV])
        v_tail = sb("v_tail", [META, HEADS, DV])
        kd_tok = sb("kd_tok", [P, 2, NCH, CH])
        state = sb("state", [P, 2, NCH, DV])
        s_r = sb("s_r", [P, HEADS, T])
        glr = sb("glr", [2 * RANK, T])

        PS = [ctx.enter_context(nc.psum_tensor(f"PS{i}", [P, 2, 512], F32)) for i in range(4)]

        def pair(i, span=ALL):
            return PS[i][:, 0:span[2], 0:span[1]]

        def rank_weights():
            return par[:, C_GL:C_ALL].rearrange("p (k r) -> p k r", r=RANK)

        def halves(ap, span=ALL):
            return ap[:, span[0]:T].rearrange("p (a b) -> p a b", a=span[2])

        def part(i, span, p):
            return PS[i][:, p, 0:halved(span)[1]]

        def tokens(span, p):
            n = halved(span)[1]
            return slice(span[0] + p * n, span[0] + (p + 1) * n)

        def matmul_parts(ps, span):
            first, n, count = span
            return [(PS[ps][:, i, 0:n], slice(first + i * n, first + (i + 1) * n)) for i in range(count)]

        names = """par_loaded consts consts_dve masks raw_hi split_done piece_done out_stored setup row_sync silu_done
            prod_done h_hi_done h_lo_done down_evac resid_done sq_done s1_done s2_done mean_acc msq_acc
            mean_sq_done var_done std_done rstd_done mean_done mean_copied mean_spread rstd_spread diag_done
            pool_centered rank_hi_done rank_lo_done acc_first resid_first s1_first sq_first s2_first mean_first
            mean_first_copied centered_first diag_first rstd_first xhat_first x_hi_first centered xhat_done
            x_hi_done x_full_done x_lo_done warm_done pw_acc out_acc qkv_evac u_evac w_evac sr_evac wop_evac
            glr_acc glr_done z_acc zb_done abs_done en_done ln_done b_step b_done arg_done exp_done qe_done
            kdec_done ktqt_done lev_acc lev_evac diag_acc diag_evac tdiag_acc vtr_acc v_tok_done v_tail_done
            ktr_acc kd_tok_done u_acc s_step s_done pool_step pool_done wsplit_step o_acc o_done osq_done ms_acc
            rms_std rms_inv rms_spread o_scaled o_fin o_hi_done o_lo_done""".split()
        S = {n: sem(n) for n in names}
        x_loaded = [sem(f"x_loaded{k}") for k in range(KC)]
        first_full = [sem(f"first_full{i}") for i in range(SLOTS)]
        raw_full = [sem(f"raw_full{i}") for i in range(RAWS)]
        block = ctx.enter_context(nc.Block())

        LN_PER = 3

        def wait_stream(eng, l, idx):
            name, value = stream_ready(l, idx)
            eng.wait_ge(S[name], value)

        @block.sync
        def _(sp):
            for kind, n in START_ORDER:
                if kind == "piece":
                    sp.dma_start(raw_first[:, n, :], stream[n // RAWS, n % RAWS]).then_inc(first_full[n], 16)
                elif n > 0:
                    sp.dma_start(X[:, n, :], x_t[n * P:(n + 1) * P, :]).then_inc(x_loaded[n], 16)
            for n in range(RAWS):
                sp.dma_start(raw[:, n, :], stream[SLOTS // RAWS, n]).then_inc(raw_full[n], 16)
            with sp.Fori(SLOTS // RAWS + 1, DEPTH * LAYER_PIECES // RAWS) as i:
                for n in range(RAWS):
                    sp.wait_ge(S["split_done"], i * RAWS + (n - RAWS + 1))
                    sp.dma_start(raw[:, n, :], stream[i, n]).then_inc(raw_full[n], 16)
            for k in range(KC):
                sp.wait_ge(S["x_full_done"], DEPTH * LN_PER * KC - KC + k + 1)
                sp.dma_start(out_t[k * P:(k + 1) * P, :], X[:, k, META:T]).then_inc(S["out_stored"], 16)
            sp.wait_ge(S["out_stored"], 16 * KC)

        @block.gpsimd
        def _(pool):
            def split(slot, done):
                pool.wait_ge(S["raw_hi"], done)
                nc.gpsimd.tensor_tensor(w_lo[:, slot, :], raw[:, slot % RAWS, :], w_hi[:, slot, :].bitcast(F32),
                                        ALU.subtract).then_inc(S["split_done"], 1)

            nc.gpsimd.memset(level_mask[:, :, :], 1).then_inc(S["consts"], 1)
            nc.gpsimd.memset(ident_mask[:, :], 0).then_inc(S["consts"], 1)
            nc.gpsimd.memset(ident[:, :], 0.0).then_inc(S["consts"], 1)
            pool.wait_ge(S["consts"], 3)
            n = 3
            for m in (ident_mask, ident):
                nc.gpsimd.affine_select(out=m[:, :], in_=m[:, :], compare_op=ALU.not_equal, fill=1.0, base=0,
                                        pattern=[[-1, P]], channel_multiplier=1).then_inc(S["consts"], 1)
            n += 2
            for i, s in enumerate(LEVELS):
                m = level_mask[:, i, :].rearrange("p (b s) -> p b s", s=s)
                nb = CH // 2 // s
                nc.gpsimd.affine_select(out=m, in_=m, compare_op=ALU.is_ge, fill=0.0, base=0,
                                        pattern=[[-2 * s, nb], [0, s]], channel_multiplier=1).then_inc(S["consts"], 1)
                n += 1
                pool.wait_ge(S["consts"], n)
                nc.gpsimd.affine_select(out=m, in_=m, compare_op=ALU.is_ge, fill=0.0, base=s - 1,
                                        pattern=[[2 * s, nb], [0, s]], channel_multiplier=-1).then_inc(S["consts"], 1)
                n += 1
                pool.wait_ge(S["consts"], n)
            nc.gpsimd.memset(acc_t[:, :, :], 0.0).then_inc(S["masks"], 1)
            with pool.Fori(1, DEPTH * LAYER_PIECES // SLOTS) as i:
                for n in range(SLOTS):
                    split(n, i * SLOTS + (n + 1))
            pool.wait_ge(S["mean_first_copied"], DEPTH * LN_PER)
            pool.wait_ge(S["mean_copied"], DEPTH * LN_PER)
            for k in range(DVE_CENTERS, KC):
                nc.gpsimd.tensor_tensor(X[:, k, META:T], X[:, k, META:T], mean[:, META:T],
                                        ALU.subtract).then_inc(S["pool_centered"], 1)

        @block.tensor
        def _(pe):
            def tile_products(o, tok, slot, t, k, rhs_hi, rhs_lo, first, last):
                hi = w_hi[:, slot, t * P:(t + 1) * P]
                lo = w_lo[:, slot, t * P:(t + 1) * P]
                nc.tensor.matmul(o, hi, rhs_hi[:, k, tok], start=first, stop=False)
                nc.tensor.matmul(o, hi, rhs_lo[:, k, tok], start=False, stop=False)
                return nc.tensor.matmul(o, lo, rhs_hi[:, k, tok], start=False, stop=last)

            def chunk_products(LN, k, n, pieces, span=ALL):
                hi = [w_hi[:, j, k * P:(k + 1) * P] for j in range(n)]
                lo = [w_lo[:, j, k * P:(k + 1) * P] for j in range(n)]

                def with_high(j, o, tok):
                    nc.tensor.matmul(o, hi[j], x_hi[:, k, tok], start=k == 0, stop=False)
                    nc.tensor.matmul(o, lo[j], x_hi[:, k, tok], start=False, stop=False)

                if k == 0:
                    pe.wait_ge(S["x_hi_first"], LN + 1)
                    if span == OWN:
                        pe.wait_ge(S["x_hi_done"], LN * KC + 1)
                    for i in range(span[2]):
                        if i == 1:
                            pe.wait_ge(S["x_hi_done"], LN * KC + 1)
                        for j in range(n):
                            if i == 0:
                                pe.wait_ge(S["split_done"], pieces + (j + 1))
                            with_high(j, *matmul_parts(j, span)[i])
                else:
                    pe.wait_ge(S["x_hi_done"], LN * KC + (k + 1))
                    for j in range(n):
                        for o, tok in matmul_parts(j, span):
                            with_high(j, o, tok)
                pe.wait_ge(S["x_lo_done"], LN * KC + (k + 1))
                for j in range(n):
                    for o, tok in matmul_parts(j, span):
                        m = nc.tensor.matmul(o, hi[j], x_lo[:, k, tok], start=False, stop=k == KC - 1)
                    if k == KC - 1:
                        m.then_inc(S["piece_done"], 1)

            def product(ps, slot, rhs_hi, rhs_lo, n, t0=0, span=ALL):
                for k in range(n):
                    for o, tok in matmul_parts(ps, span):
                        m = tile_products(o, tok, slot, t0 + k, k, rhs_hi, rhs_lo, k == 0, k == n - 1)
                return m

            def last_product(ps, slot, rhs_hi, rhs_lo, n, t0, span):
                for p, (o, tok) in enumerate(matmul_parts(ps, halved(span))):
                    for k in range(n):
                        m = tile_products(o, tok, slot, t0 + k, k, rhs_hi, rhs_lo, k == 0, k == n - 1)
                    m.then_inc(S["acc_first" if p == 0 else "piece_done"], 1)

            def ffn(l, f, span):
                F22, FP, FD = l * 44 + 22 * f, l * LAYER_PIECES + f * (FFN_PIECES + MIX_IN + MIX_OUT), \
                    l * 32 + 16 * f
                LN = l * LN_PER + 2 * f
                piece = 0
                for p, (m0, nm) in enumerate(PHASES):
                    last_phase = p == len(PHASES) - 1

                    def gate_up(i, first, base):
                        for j in range(4):
                            m = i * 2 + (m0 + j // 2)
                            pe.wait_ge(S["split_done"], FP + i * 4 + (base + j + 1))
                            if not first:
                                pe.wait_ge(S["silu_done" if j % 2 == 0 else "prod_done"], F22 + m - 1)
                            elif p > 0:
                                pe.wait_ge(S["down_evac"], FD + (8 * (p - 1) + 4 + j + 1))
                            product(j, j, x_hi, x_lo, KC, span=span).then_inc(S["piece_done"], 1)

                    if p == 0:
                        for k in range(KC):
                            chunk_products(LN, k, 3, FP, span)
                        pe.wait_ge(S["split_done"], FP + 4)
                        product(3, 3, x_hi, x_lo, KC, span=span).then_inc(S["piece_done"], 1)
                    else:
                        gate_up(0, True, piece)
                    with pe.Fori(1, nm // 2) as i:
                        gate_up(i, False, piece)
                    piece += 2 * nm
                    for mo in range(KC):
                        j = mo % 4
                        pe.wait_ge(S["split_done"], FP + (piece + mo + 1))
                        if mo < 4:
                            pe.wait_ge(S["silu_done" if j % 2 == 0 else "prod_done"],
                                       F22 + (m0 + nm - 1 + mo // 2))
                        elif last_phase:
                            pe.wait_ge(S["resid_done"], LN * KC + (mo - 3))
                        else:
                            pe.wait_ge(S["down_evac"], FD + (8 * p + mo - 3))
                        if last_phase and mo == KC - 1:
                            last_product(j, (piece + mo) % 4, h_hi, h_lo, nm, 0, span)
                            break
                        for k in range(nm):
                            if mo == 0:
                                pe.wait_ge(S["h_lo_done"], F22 + (m0 + k + 1))
                            for o, tok in matmul_parts(j, span):
                                m = tile_products(o, tok, (piece + mo) % 4, k, k, h_hi, h_lo, k == 0, k == nm - 1)
                        m.then_inc(S["piece_done"], 1)
                    piece += KC

            def ln_stats(LN, span):
                n_tok, blocks = stat_blocks(span)

                def columns(bank, sums, p):
                    for c in range(p * blocks // 2, (p + 1) * blocks // 2):
                        tok = slice(span[0] + c * n_tok, span[0] + (c + 1) * n_tok)
                        m = nc.tensor.matmul(PS[0][0:n_tok, bank, c:c + 1], sums[:, tok], ones_mean[:, 0:1],
                                             start=True, stop=True)
                    return m

                def spread_mean(p):
                    return nc.tensor.matmul(part(1, span, p), ones_mean[:, :], sum_x[:, tokens(span, p)],
                                            start=True, stop=True)

                def spread_rstd(p):
                    return nc.tensor.matmul(part(3, span, p), ones[0:n_tok, :], diag[0:n_tok, tokens(span, p)],
                                            start=True, stop=True)

                pe.wait_ge(S["masks"], 1)
                pe.wait_ge(S["consts_dve"], 1)
                pe.wait_ge(S["resid_first"], LN + 1)
                pe.wait_ge(S["s1_first"], LN + 1)
                columns(0, sum_x, 0)
                pe.wait_ge(S["s2_first"], LN + 1)
                columns(1, sum_sq, 0)
                spread_mean(0).then_inc(S["mean_first"], 1)
                pe.wait_ge(S["s1_done"], LN * 7 + 7)
                columns(0, sum_x, 1).then_inc(S["mean_acc"], 1)
                pe.wait_ge(S["s2_done"], LN * 7 + 7)
                columns(1, sum_sq, 1).then_inc(S["msq_acc"], 1)
                pe.wait_ge(S["resid_done"], LN * KC + KC)
                spread_mean(1).then_inc(S["mean_spread"], 1)
                pe.wait_ge(S["diag_first"], LN + 1)
                spread_rstd(0).then_inc(S["rstd_first"], 1)
                pe.wait_ge(S["diag_done"], LN + 1)
                spread_rstd(1).then_inc(S["rstd_spread"], 1)

            def group_free(l, idx):
                kind, n = GROUPS_ORDER[idx]
                at = {"q": ("qkv_evac", 8, n), "k": ("qkv_evac", 8, 2 + n), "v": ("qkv_evac", 8, 4 + n),
                      "u": ("u_evac", 4, n), "w": ("w_evac", 4, n), "r": ("sr_evac", 4, n),
                      "p": ("wop_evac", 8, n)}.get(kind)
                if kind == "g":
                    pe.wait_ge(S["resid_done"], l * 24 + (8 + n + 1))
                else:
                    pe.wait_ge(S[at[0]], l * at[1] + (at[2] + 1))

            def mixer(l, span):
                FP = l * LAYER_PIECES + FFN_PIECES
                LN = l * LN_PER + 1
                pe.wait_ge(S["par_loaded"], l * 16 + 16)
                pe.wait_ge(S["rank_lo_done"], l + 1)
                for k in range(KC):
                    chunk_products(LN, k, 2, FP)
                    for half in range(2):
                        for x in (x_hi, x_lo):
                            m = nc.tensor.matmul(PS[2][0:2 * RANK, half, 0:HALF], w_rank[:, k, :],
                                                 x[:, k, half * HALF:(half + 1) * HALF],
                                                 start=k == 0 and x is x_hi, stop=k == KC - 1 and x is x_lo)
                m.then_inc(S["glr_acc"], 1)
                pieces = [2]

                def project(idx, span=ALL):
                    pe.wait_ge(S["split_done"], FP + (pieces[0] + 1))
                    group_free(l, idx - 2)
                    product(idx % 2, pieces[0] % 4, x_hi, x_lo, KC, span=span).then_inc(S["piece_done"], 1)
                    pieces[0] += 1

                def pool_product(idx, g):
                    pe.wait_ge(S["pool_done"], l * 4 + (g + 1))
                    group_free(l, idx - 2)
                    for half in range(2):
                        m = nc.tensor.matmul(PS[idx % 2][:, half, 0:HALF], par[:, C_WP + g * P:C_WP + (g + 1) * P],
                                             ft[:, g % 2, half * HALF:(half + 1) * HALF], start=True, stop=True)
                    m.then_inc(S["pw_acc"], 1)

                def gate_logits():
                    pe.wait_ge(S["glr_done"], l + 1)
                    for t in range(2):
                        for half in range(2):
                            m = nc.tensor.matmul(PS[2 + t][:, half, 0:HALF],
                                                 par[0:2 * RANK, C_GU + t * P:C_GU + (t + 1) * P],
                                                 glr[:, half * HALF:(half + 1) * HALF], start=True, stop=True)
                        m.then_inc(S["z_acc"], 1)

                def rows(h):
                    return slice((h % 2) * DK, (h % 2 + 1) * DK)

                def by_row_tiles():
                    return [(2 * hp + odd, c) for hp in range(2) for c in range(NCH) for odd in range(2)]

                def even_tails(product):
                    product(0)
                    product(2).then_inc(S["row_sync"], 1)

                def odd_tails(product):
                    product(1)
                    return product(3)

                def diagonal():
                    pe.wait_ge(S["qkv_evac"], l * 8 + 4)
                    pe.wait_ge(S["zb_done"], l * 2 + 2)
                    for h, c in by_row_tiles():
                        tok = slice(c * CH, (c + 1) * CH)
                        m = nc.tensor.matmul(PS[2 + h % 2][:, h // 2, tok], qk[rows(h), 2 + h // 2, tok],
                                             qk[rows(h), h // 2, tok], start=True, stop=True)
                    m.then_inc(S["diag_acc"], 1)

                def tail_diagonal(h):
                    return nc.tensor.matmul(PS[3][0:META, 0, place(h) * META:(place(h) + 1) * META],
                                            qk[rows(h), 2 + h // 2, TAIL:T], qk[rows(h), h // 2, TAIL:T],
                                            start=True, stop=True)

                def v_transpose(h):
                    pe.wait_ge(S["qkv_evac"], l * 8 + (4 + h + 1))
                    if h > 0:
                        pe.wait_ge(S["v_tok_done"], l * 4 + h)
                        pe.wait_ge(S["v_tail_done"], l * 4 + h)
                    for c in range(NCH):
                        nc.tensor.transpose(PS[3][:, 1, c * CH:(c + 1) * CH], ft[:, h % 2, c * CH:(c + 1) * CH], ident[:, :])
                    nc.tensor.transpose(PS[3][0:META, 0, 256:256 + DV], ft[:, h % 2, TAIL:T],
                                        ident[:, :]).then_inc(S["vtr_acc"], 1)

                def k_transpose(t):
                    pe.wait_ge(S["kdec_done"], l + 1)
                    if t == 0:
                        pe.wait_ge(S["v_tok_done"], l * 4 + 4)
                    else:
                        pe.wait_ge(S["kd_tok_done"], l * 2 + 1)
                    for c in range(NCH):
                        m = nc.tensor.transpose(PS[3][:, 1, c * CH:(c + 1) * CH], kdec[:, t, c * CH:(c + 1) * CH], ident[:, :])
                    m.then_inc(S["ktr_acc"], 1)

                def level(i):
                    s = LEVELS[i]
                    if i == 0:
                        pe.wait_ge(S["diag_evac"], l * 2 + 2)
                    else:
                        pe.wait_ge(S["lev_evac"], l * 7 + i)
                    if s <= META // 2:
                        pe.wait_ge(S["v_tail_done"], l * 4 + 4)
                    pe.wait_ge(S["ktqt_done"], l * 7 + (i + 1))
                    tail = s <= META // 2

                    def tail_level(h):
                        return nc.tensor.matmul(PS[3][0:META, 0, place(h) * 8:(place(h) + 1) * 8],
                                                kt[rows(h), i % 2, h // 2, TAIL:T], qt[rows(h), i % 2, h // 2, 256:264],
                                                start=True, stop=True)

                    if tail:
                        even_tails(tail_level)
                    for h, c in by_row_tiles():
                        m = nc.tensor.matmul(PS[2][:, h % 2, (h // 2) * 256 + c * 64:(h // 2) * 256 + (c + 1) * 64],
                                             kt[rows(h), i % 2, h // 2, c * CH:(c + 1) * CH],
                                             qt[rows(h), i % 2, h // 2, c * 64:(c + 1) * 64], start=True, stop=True)
                    if tail:
                        pe.wait_ge(S["row_sync"], l * 5 + (i - 1))
                        m = odd_tails(tail_level)
                    m.then_inc(S["lev_acc"], 1)

                def chunk_updates(t):
                    pe.wait_ge(S["kd_tok_done"], l * 2 + 2)
                    if t == 1:
                        pe.wait_ge(S["s_done"], l * 2 + 1)
                    pe.wait_ge(S["consts_dve"], 1)
                    for h in (2 * t, 2 * t + 1):
                        for c in range(NCH):
                            m = nc.tensor.matmul(PS[3][rows(h), 1, c * DV:(c + 1) * DV], kd_tok[:, t, c, rows(h)],
                                                 v_tok[:, h, c, :], start=True, stop=True)
                    m.then_inc(S["u_acc"], 1)

                def attend(h):
                    ps = 2 + h % 2
                    if h < 2:
                        pe.wait_ge(S["lev_evac"], l * 7 + 7)
                        pe.wait_ge(S["s_done"], l * 2 + 2)
                    else:
                        pe.wait_ge(S["o_done"], l * 4 + (h - 1))
                    for c in range(NCH):
                        tok = slice(c * CH, (c + 1) * CH)
                        if c > 0:
                            nc.tensor.matmul(PS[ps][:, 0, tok], state[rows(h), h // 2, c - 1, :], qe[rows(h), h // 2, tok],
                                             start=True, stop=False)
                        nc.tensor.matmul(PS[ps][:, 0, tok], v_tok[:, h, c, :], acc_a[:, place(h), c, :], start=c == 0, stop=True)
                    nc.tensor.matmul(PS[ps][:, 1, 0:META], state[rows(h), h // 2, NCH - 1, :], qe[rows(h), h // 2, TAIL:T],
                                     start=True, stop=False)
                    nc.tensor.matmul(PS[ps][:, 1, 0:META], v_tail[:, h, :], acc_t[:, place(h), :], start=False,
                                     stop=True).then_inc(S["o_acc"], 1)

                first, n_quarter = span[0], (T - span[0]) // QUARTERS

                def mean_squares():
                    pe.wait_ge(S["osq_done"], l * 4 + 4)
                    pe.wait_ge(S["o_done"], l * 4 + 4)
                    for h in range(HEADS):
                        for q in range(QUARTERS):
                            row = h * QUARTERS + q
                            tok = slice(first + q * n_quarter, first + (q + 1) * n_quarter)
                            m = nc.tensor.matmul(PS[2][0:RMS_ROWS, 0, 0:n_quarter],
                                                 rms_comb[:, RMS_ROWS - 1 - row:2 * RMS_ROWS - 1 - row],
                                                 ex[:, h, tok], start=row == 0, stop=row == RMS_ROWS - 1)
                    m.then_inc(S["ms_acc"], 1)

                def spread_rms(h):
                    pe.wait_ge(S["masks"], 1)
                    pe.wait_ge(S["rms_inv"], l + 1)
                    if h >= 2:
                        pe.wait_ge(S["o_scaled"], l * 4 + (h - 1))
                    for q in range(QUARTERS):
                        row = h * QUARTERS + q
                        bank, at = divmod(q * n_quarter, span[1])
                        m = nc.tensor.matmul(PS[2 + h % 2][:, bank, at:at + n_quarter],
                                             ident[0:RMS_ROWS, row:row + 1].to_broadcast([RMS_ROWS, P]),
                                             rms_rows[:, 0:n_quarter], start=True, stop=True)
                    m.then_inc(S["rms_spread"], 1)

                def out_product(idx, mo, part, rhs_hi, rhs_lo):
                    piece = MIX_IN + part * 4 + mo // 2
                    if mo % 2 == 0:
                        pe.wait_ge(S["split_done"], FP + (piece + 1))
                    group_free(l, idx - 2)
                    if part == 1 and mo == KC - 1:
                        last_product(idx % 2, piece % 4, rhs_hi, rhs_lo, 4, 4, span)
                        return
                    m = product(idx % 2, piece % 4, rhs_hi, rhs_lo, 4, 4 * (mo % 2), span)
                    m.then_inc(S["out_acc" if mo % 2 == 0 else "piece_done"], 1)

                project(2)
                gate_logits()
                project(3)
                project(4)
                diagonal()
                project(5)
                pe.wait_ge(S["masks"], 1)
                pe.wait_ge(S["diag_evac"], l * 2 + 2)
                even_tails(tail_diagonal)
                pe.wait_ge(S["row_sync"], l * 5 + 1)
                v_transpose(0)
                odd_tails(tail_diagonal).then_inc(S["tdiag_acc"], 1)
                project(6)
                level(0)
                v_transpose(1)
                project(7)
                level(1)
                v_transpose(2)
                project(8)
                level(2)
                v_transpose(3)
                project(9)
                pool_product(10, 0)
                level(3)
                k_transpose(0)
                project(11)
                pool_product(12, 1)
                level(4)
                k_transpose(1)
                project(13)
                pool_product(14, 2)
                level(5)
                project(15, span)
                pool_product(16, 3)
                level(6)
                chunk_updates(0)
                project(17, span)
                chunk_updates(1)
                project(18, span)
                attend(0)
                attend(1)
                project(19, span)
                attend(2)
                attend(3)
                pe.wait_ge(S["w_evac"], l * 4 + 4)
                for mo in range(8):
                    out_product(20 + mo, mo, 0, yp_hi, yp_lo)
                    if mo == 1:
                        mean_squares()
                    if mo in (3, 5):
                        spread_rms(mo - 3)
                        spread_rms(mo - 2)
                pe.wait_ge(S["o_lo_done"], l * 4 + 4)
                for mo in range(8):
                    out_product(28 + mo, mo, 1, x_hi, x_lo)

            def layer(l, span):
                ffn(l, 0, ALL)
                ln_stats(l * LN_PER, ALL)
                mixer(l, span)
                ln_stats(l * LN_PER + 1, span)
                ffn(l, 1, span)
                ln_stats(l * LN_PER + 2, span)

            with pe.Fori(0, DEPTH - 1) as l:
                layer(l, ALL)
            layer(DEPTH - 1, OWN)

        @block.scalar
        def _(act):
            def ffn(l, f, span):
                F22 = l * 44 + 22 * f
                n = f * (FFN_PIECES + MIX_IN + MIX_OUT)
                for m in range(MT):
                    phase = max(p for p, (m0, _) in enumerate(PHASES) if m0 <= m)
                    act.wait_ge(S["piece_done"], gate_piece(l, f, m))
                    nc.scalar.activation(halves(silu, span), pair(2 * (m % 2), span), ACT.Silu).then_inc(S["silu_done"], 1)
                    high(l, n + SLOTS)
                    act.wait_ge(S["prod_done"], F22 + (m + 1))
                    nc.scalar.activation(h_hi[:, m - PHASES[phase][0], span[0]:T], prod[:, span[0]:T], ACT.Copy).then_inc(S["h_hi_done"], 1)
                    high(l, n + 1 + SLOTS)
                    n += 2
                    if m == sum(PHASES[phase]) - 1 and m < MT - 1:
                        for mo in range(KC):
                            high(l, n + SLOTS)
                            n += 1
                if f == 0:
                    act.wait_ge(S["par_loaded"], l * 16 + 16)
                    nc.scalar.activation(w_rank[:, :, 0:RANK], rank_weights(), ACT.Copy).then_inc(S["rank_hi_done"], 1)
                squares(l, 2 * f, n, 1, span)

            def high(l, n):
                if n >= LAYER_PIECES and type(l) is int and l == DEPTH - 1:
                    return
                act.wait_ge(S["piece_done"], l * LAYER_PIECES + (n - SLOTS + 1))
                act.wait_ge(raw_full[n % RAWS], l * (16 * LAYER_PIECES // RAWS) + 16 * ((n - SLOTS) // RAWS + 1))
                nc.scalar.activation(w_hi[:, n % SLOTS, :], raw[:, n % RAWS, :], ACT.Copy).then_inc(S["raw_hi"], 1)

            def squares(l, r, n, per_piece, span):
                LN = l * LN_PER + r
                act.wait_ge(S["consts_dve"], 1)
                nc.scalar.activation(warm[:, 1:2], warm[:, 0:1], ACT.Sqrt).then_inc(S["warm_done"], 1)
                for k in range(KC):
                    if k == KC - 1:
                        act.wait_ge(S["resid_first"], LN + 1)
                        act.wait_ge(S["s2_done"], LN * 7 + (k - 2))
                        tok = tokens(span, 0)
                        nc.scalar.activation(sq[:, k % 2, tok], X[:, k, tok], ACT.Square).then_inc(S["sq_first"], 1)
                        tok = tokens(span, 1)
                    else:
                        tok = slice(span[0], T)
                    act.wait_ge(S["resid_done"], LN * KC + (k + 1))
                    if 2 <= k < KC - 1:
                        act.wait_ge(S["s2_done"], LN * 7 + max(k - 2, 1))
                    nc.scalar.activation(sq[:, k % 2, tok], X[:, k, tok], ACT.Square).then_inc(S["sq_done"], 1)
                    if (k + 1) % per_piece == 0 and k < KC - 1:
                        high(l, n + SLOTS)
                        n += 1

            def norm(l, r, n, span, final=False):
                LN = l * LN_PER + r
                act.wait_ge(S["par_loaded"], l * 16 + 16)

                def copy_mean(p):
                    return nc.scalar.activation(mean[:, tokens(span, p)], part(1, span, p), ACT.Copy)

                act.wait_ge(S["mean_first"], LN + 1)
                copy_mean(0).then_inc(S["mean_first_copied"], 1)
                act.wait_ge(S["var_done"], LN + 1)
                n_tok, blocks = stat_blocks(span)
                nc.scalar.activation(col_std[0:n_tok, 0:blocks], col_var[0:n_tok, 0:blocks], ACT.Sqrt)\
                    .then_inc(S["std_done"], 1)
                act.wait_ge(S["mean_spread"], LN + 1)
                copy_mean(1).then_inc(S["mean_copied"], 1)
                g = C_LN + 16 * r

                def affine(out, k, tok):
                    normed = X[:, k, tok] if final else xhat[:, k % 2, tok]
                    return nc.scalar.activation(out[:, k, tok], normed, ACT.Identity, bias=par[:, g + 8 + k:g + 9 + k],
                                                scale=par[:, g + k:g + k + 1])

                for k in range(KC):
                    tok = slice(span[0], T)
                    if k == 0:
                        act.wait_ge(S["xhat_first"], LN + 1)
                        if not final:
                            affine(x_hi, 0, tokens(span, 0)).then_inc(S["x_hi_first"], 1)
                            tok = tokens(span, 1)
                    act.wait_ge(S["xhat_done"], LN * KC + (k + 1))
                    if not final:
                        affine(x_hi, k, tok).then_inc(S["x_hi_done"], 1)
                    affine(X, k, slice(span[0], T)).then_inc(S["x_full_done"], 1)
                    if k == 0:
                        high(l, n + SLOTS)

            def mixer(l, span):
                def evac(idx, out, scale=1.0):
                    wait_stream(act, l, idx)
                    nc.scalar.activation(halves(out), pair(idx % 2), ACT.Copy, scale=scale).then_inc(S["qkv_evac"], 1)

                def exp_of(i):
                    act.wait_ge(S["arg_done"], l * 8 + (i + 2))
                    e = ex[:, 2 * (i % 2):2 * (i % 2) + 2, :] if LEVELS[i] <= META // 2 else \
                        ex[:, 2 * (i % 2):2 * (i % 2) + 2, 0:SEQ]
                    nc.scalar.activation(e, e, ACT.Exp, scale=1.0 / GATE_TEMP).then_inc(S["exp_done"], 1)

                def v_to_tokens(h):
                    act.wait_ge(S["vtr_acc"], l * 4 + (h + 1))
                    nc.scalar.activation(v_tok[:, h, :, :].rearrange("p c d -> p (c d)"), PS[3][:, 1, :],
                                         ACT.Copy).then_inc(S["v_tok_done"], 1)

                def k_to_tokens(t):
                    act.wait_ge(S["ktr_acc"], l * 2 + (t + 1))
                    nc.scalar.activation(kd_tok[:, t, :, :].rearrange("p c d -> p (c d)"), PS[3][:, 1, :],
                                         ACT.Copy).then_inc(S["kd_tok_done"], 1)

                n0 = FFN_PIECES + SLOTS
                evac(0, qk[:, 0, :], DK ** -0.5)
                evac(1, qk[:, 1, :], DK ** -0.5)
                high(l, n0)
                high(l, n0 + 1)
                evac(2, qk[:, 2, :])
                high(l, n0 + 2)
                for t in range(2):
                    act.wait_ge(S["z_acc"], l * 2 + (t + 1))
                    nc.scalar.activation(halves(bcum[:, t, :]), pair(2 + t), ACT.Identity,
                                         bias=par[:, C_BG + t:C_BG + t + 1]).then_inc(S["zb_done"], 1)
                act.wait_ge(S["abs_done"], l + 1)
                nc.scalar.activation(ex[:, 0:2, :], ex[:, 0:2, :], ACT.Exp, scale=-1.0).then_inc(S["en_done"], 1)
                act.wait_ge(S["en_done"], l + 1)
                nc.scalar.activation(ex[:, 0:2, :], ex[:, 0:2, :], ACT.Ln, bias=1.0).then_inc(S["ln_done"], 1)
                evac(3, qk[:, 3, :])
                high(l, n0 + 3)
                act.wait_ge(S["b_done"], l + 1)
                nc.scalar.activation(ex[:, 0:2, :], bcum[:, :, :], ACT.Exp, scale=1.0 / GATE_TEMP).then_inc(S["exp_done"], 1)
                act.wait_ge(S["arg_done"], l * 8 + 1)
                nc.scalar.activation(ex[:, 2:4, 0:SEQ], ex[:, 2:4, 0:SEQ], ACT.Exp,
                                     scale=1.0 / GATE_TEMP).then_inc(S["exp_done"], 1)
                evac(4, ft[:, 0, :])
                high(l, n0 + 4)
                exp_of(0)
                evac(5, ft[:, 1, :])
                high(l, n0 + 5)
                exp_of(1)
                v_to_tokens(0)
                exp_of(2)
                evac(6, ft[:, 0, :])
                high(l, n0 + 6)
                v_to_tokens(1)
                exp_of(3)
                evac(7, ft[:, 1, :])
                high(l, n0 + 7)
                v_to_tokens(2)
                exp_of(4)
                high(l, n0 + 8)
                v_to_tokens(3)
                exp_of(5)
                high(l, n0 + 9)
                k_to_tokens(0)
                exp_of(6)
                high(l, n0 + 10)
                k_to_tokens(1)
                high(l, n0 + 11)
                for h, idx in enumerate((15, 17, 18, 19)):
                    wait_stream(act, l, idx)
                    nc.scalar.activation(halves(s_r[:, h, :], span), pair(idx % 2, span), ACT.Silu).then_inc(S["sr_evac"], 1)
                    high(l, n0 + 12 + h)
                for h in range(HEADS):
                    act.wait_ge(S["o_done"], l * 4 + (h + 1))
                    nc.scalar.activation(ex[:, h, :], qk[:, h, :], ACT.Square).then_inc(S["osq_done"], 1)

                def o_high(h):
                    act.wait_ge(S["o_fin"], l * 4 + (h + 1))
                    nc.scalar.activation(x_hi[:, h, span[0]:T], qk[:, h, span[0]:T], ACT.Copy).then_inc(S["o_hi_done"], 1)

                high(l, n0 + 16)
                act.wait_ge(S["ms_acc"], l + 1)
                n_quarter = (T - span[0]) // QUARTERS
                nc.scalar.activation(rms_rows[:, 0:n_quarter], PS[2][0:RMS_ROWS, 0, 0:n_quarter], ACT.Sqrt,
                                     bias=rms_eps[0:RMS_ROWS, :]).then_inc(S["rms_std"], 1)
                high(l, n0 + 17)
                o_high(0)
                o_high(1)
                high(l, n0 + 18)
                o_high(2)
                o_high(3)
                high(l, n0 + 19)
                squares(l, 1, FFN_PIECES + 20, 2, span)

            act.dma_start(X[:, 0, :], x_t[0:P, :]).then_inc(x_loaded[0], 16)
            act.wait_ge(S["setup"], 1)
            nc.scalar.activation(warm[:, 1:2], warm[:, 0:1], ACT.Silu).then_inc(S["warm_done"], 1)
            for kind, n in START_ORDER:
                if kind == "piece":
                    act.wait_ge(first_full[n], 16)
                    nc.scalar.activation(w_hi[:, n, :], raw_first[:, n, :], ACT.Copy).then_inc(S["raw_hi"], 1)
                else:
                    act.wait_ge(x_loaded[n], 16)
                    tok = slice(0, T)
                    if n == 0:
                        nc.scalar.activation(x_hi[:, 0, 0:HALF], X[:, 0, 0:HALF], ACT.Copy).then_inc(S["x_hi_first"], 1)
                        tok = slice(HALF, T)
                    nc.scalar.activation(x_hi[:, n, tok], X[:, n, tok], ACT.Copy).then_inc(S["x_hi_done"], 1)
            act.dma_start(par[:, :], params[0]).then_inc(S["par_loaded"], 16)

            def layer(l, span):
                ffn(l, 0, ALL)
                norm(l, 0, FFN_PIECES - 1, ALL)
                mixer(l, span)
                norm(l, 1, FFN_PIECES + MIX_IN + MIX_OUT - 1, span)
                ffn(l, 1, span)
                norm(l, 2, LAYER_PIECES - 1, span, final=span == OWN)

            with act.Fori(0, DEPTH - 1) as l:
                layer(l, ALL)
                act.wait_ge(S["x_full_done"], l * 24 + 24)
                act.dma_start(par[:, :], params[l + 1]).then_inc(S["par_loaded"], 16)
            layer(DEPTH - 1, OWN)

        @block.vector
        def _(dve):
            V = nc.vector

            def ffn(l, f, span):
                F22 = l * 44 + 22 * f
                for p, (m0, nm) in enumerate(PHASES):
                    for m in range(m0, m0 + nm):
                        dve.wait_ge(S["silu_done"], F22 + (m + 1))
                        dve.wait_ge(S["piece_done"], gate_piece(l, f, m) + 1)
                        if m > 0:
                            dve.wait_ge(S["h_lo_done"], F22 + m)
                        V.scalar_tensor_tensor(out=halves(prod, span), in0=pair(2 * (m % 2) + 1, span), scalar=0.5,
                                               in1=halves(silu, span), op0=ALU.mult, op1=ALU.mult).then_inc(S["prod_done"], 1)
                        dve.wait_ge(S["h_hi_done"], F22 + (m + 1))
                        V.tensor_tensor(h_lo[:, m - m0, span[0]:T], prod[:, span[0]:T], h_hi[:, m - m0, span[0]:T].bitcast(F32),
                                        ALU.subtract).then_inc(S["h_lo_done"], 1)
                    if p == len(PHASES) - 1:
                        if f == 0:
                            dve.wait_ge(S["par_loaded"], l * 16 + 16)
                            dve.wait_ge(S["rank_hi_done"], l + 1)
                            V.tensor_tensor(w_rank[:, :, RANK:2 * RANK], rank_weights(),
                                            w_rank[:, :, 0:RANK].bitcast(F32), ALU.subtract).then_inc(S["rank_lo_done"], 1)
                        resid(l * LN_PER + 2 * f, lambda mo: ("piece_done", down_piece(l, f, p, mo)), 4, span)
                        break
                    for mo in range(KC):
                        dve.wait_ge(S["piece_done"], down_piece(l, f, p, mo))
                        if p == 0:
                            V.scalar_tensor_tensor(out=halves(X[:, mo, :], span), in0=halves(X[:, mo, :], span), scalar=ALPHA,
                                                   in1=pair(mo % 4, span), op0=ALU.mult, op1=ALU.add).then_inc(S["down_evac"], 1)
                        else:
                            dve.wait_ge(S["down_evac"], l * 32 + 16 * f + 8)
                            V.tensor_tensor(halves(X[:, mo, :], span), halves(X[:, mo, :], span), pair(mo % 4, span),
                                            ALU.add).then_inc(S["down_evac"], 1)

            def resid(LN, ready, pairs, span):
                tok = slice(span[0], T)

                def add_square(k):
                    dve.wait_ge(S["sq_done"], LN * KC + (k + 1))
                    if k == 1:
                        V.tensor_tensor(sum_sq[:, tok], sq[:, 0, tok], sq[:, 1, tok], ALU.add).then_inc(S["s2_done"], 1)
                    elif k > 1:
                        dve.wait_ge(S["s2_done"], LN * 7 + (k - 1))
                        V.tensor_tensor(sum_sq[:, tok], sum_sq[:, tok], sq[:, k % 2, tok], ALU.add).then_inc(S["s2_done"], 1)

                for mo in range(KC - 1):
                    name, value = ready(mo)
                    dve.wait_ge(S[name], value)
                    V.tensor_tensor(halves(X[:, mo, :], span), halves(X[:, mo, :], span), pair(mo % pairs, span),
                                    ALU.add).then_inc(S["resid_done"], 1)
                    if mo >= 1:
                        add_square(mo - 1)
                        dve.wait_ge(S["resid_done"], LN * KC + (mo + 1))
                        if mo > 1:
                            dve.wait_ge(S["s1_done"], LN * 7 + (mo - 1))
                        V.tensor_tensor(sum_x[:, tok], X[:, 0, tok] if mo == 1 else sum_x[:, tok], X[:, mo, tok],
                                        ALU.add).then_inc(S["s1_done"], 1)
                add_square(KC - 2)
                k = KC - 1
                dve.wait_ge(S["s1_done"], LN * 7 + 6)
                for p in range(2):
                    h = tokens(span, p)
                    if p == 0:
                        dve.wait_ge(S["acc_first"], LN + 1)
                    else:
                        name, value = ready(k)
                        dve.wait_ge(S[name], value)
                    V.tensor_tensor(X[:, k, h], X[:, k, h], part(k % pairs, span, p), ALU.add)\
                        .then_inc(S["resid_done" if p else "resid_first"], 1)
                    dve.wait_ge(S["resid_done" if p else "resid_first"], LN * KC + KC if p else LN + 1)
                    V.tensor_tensor(sum_x[:, h], sum_x[:, h], X[:, k, h], ALU.add).then_inc(S["s1_done" if p else "s1_first"], 1)
                    dve.wait_ge(S["s2_done"], LN * 7 + 6)
                    dve.wait_ge(S["sq_done" if p else "sq_first"], LN * KC + KC if p else LN + 1)
                    V.tensor_tensor(sum_sq[:, h], sum_sq[:, h], sq[:, k % 2, h], ALU.add)\
                        .then_inc(S["s2_done" if p else "s2_first"], 1)

            def norm(LN, span, final=False):
                n_tok, blocks = stat_blocks(span)
                tok = slice(span[0], T)
                def center(k, h=tok):
                    out = X[:, k, h] if final else xhat[:, k % 2, h]
                    return V.tensor_tensor(out, X[:, k, h], mean[:, h], ALU.subtract)

                def scale_first(p):
                    h = tokens(span, p)
                    x = X[:, 0, h] if final else xhat[:, 0, h]
                    return V.tensor_tensor(x, x, part(3, span, p), ALU.mult)

                def scale(k):
                    x = halves(X[:, k, :] if final else xhat[:, k % 2, :], halved(span))
                    V.tensor_tensor(x, x, pair(3, halved(span)), ALU.mult).then_inc(S["xhat_done"], 1)

                def diagonals(p):
                    n = blocks // 2
                    return V.tensor_tensor(diag[0:n_tok, tokens(span, p)].rearrange("p (c i) -> p c i", i=n_tok),
                                           ident[0:n_tok, 0:n_tok].rearrange("p (o i) -> p o i", o=1)
                                           .to_broadcast([n_tok, n, n_tok]),
                                           col_rstd[0:n_tok, p * n:(p + 1) * n].rearrange("p (c o) -> p c o", o=1)
                                           .to_broadcast([n_tok, n, n_tok]), ALU.mult)

                dve.wait_ge(S["mean_acc"], LN + 1)
                V.tensor_copy(col_mean[0:n_tok, 0:blocks], PS[0][0:n_tok, 0, 0:blocks]).then_inc(S["mean_done"], 1)
                dve.wait_ge(S["mean_done"], LN + 1)
                V.tensor_tensor(col_mean_sq[0:n_tok, 0:blocks], col_mean[0:n_tok, 0:blocks], col_mean[0:n_tok, 0:blocks],
                                ALU.mult).then_inc(S["mean_sq_done"], 1)
                dve.wait_ge(S["mean_sq_done"], LN + 1)
                dve.wait_ge(S["msq_acc"], LN + 1)
                V.scalar_tensor_tensor(out=col_var[0:n_tok, 0:blocks], in0=PS[0][0:n_tok, 1, 0:blocks], scalar=LN_EPS,
                                       in1=col_mean_sq[0:n_tok, 0:blocks], op0=ALU.add, op1=ALU.subtract)\
                    .then_inc(S["var_done"], 1)
                dve.wait_ge(S["mean_first_copied"], LN + 1)
                center(0, tokens(span, 0)).then_inc(S["centered_first"], 1)
                dve.wait_ge(S["std_done"], LN + 1)
                V.reciprocal(col_rstd[0:n_tok, 0:blocks], col_std[0:n_tok, 0:blocks]).then_inc(S["rstd_done"], 1)
                dve.wait_ge(S["masks"], 1)
                dve.wait_ge(S["rstd_done"], LN + 1)
                diagonals(0).then_inc(S["diag_first"], 1)
                diagonals(1).then_inc(S["diag_done"], 1)
                dve.wait_ge(S["mean_copied"], LN + 1)
                center(0, tokens(span, 1)).then_inc(S["centered"], 1)
                if final:
                    for k in range(1, DVE_CENTERS):
                        center(k).then_inc(S["centered"], 1)
                dve.wait_ge(S["rstd_first"], LN + 1)
                dve.wait_ge(S["centered_first"], LN + 1)
                scale_first(0).then_inc(S["xhat_first"], 1)
                dve.wait_ge(S["rstd_spread"], LN + 1)
                dve.wait_ge(S["centered"], LN * KC + 1)
                scale_first(1).then_inc(S["xhat_done"], 1)
                if final:
                    for k in range(1, KC):
                        if k < DVE_CENTERS:
                            dve.wait_ge(S["centered"], LN * KC + (k + 1))
                        else:
                            dve.wait_ge(S["pool_centered"], k - DVE_CENTERS + 1)
                        scale(k)
                    return

                def lo(k):
                    dve.wait_ge(S["x_full_done"], LN * KC + (k + 1))
                    V.tensor_tensor(x_lo[:, k, tok], X[:, k, tok], x_hi[:, k, tok].bitcast(F32),
                                    ALU.subtract).then_inc(S["x_lo_done"], 1)

                center(1).then_inc(S["centered"], 1)
                for k in range(1, KC):
                    dve.wait_ge(S["centered"], LN * KC + (k + 1))
                    scale(k)
                    lo(k - 1)
                    if k < KC - 1:
                        center(k + 1).then_inc(S["centered"], 1)
                lo(KC - 1)

            def mixer(l, span):
                tok = slice(span[0], T)
                pair_exp = [ex[:, 0:2, :], ex[:, 2:4, :]]
                steps = {}

                def step(name, total, ins):
                    steps[name] = steps.get(name, 0) + 1
                    ins.then_inc(S[name], 1)
                    dve.wait_ge(S[name], l * total + steps[name])

                dve.wait_ge(S["glr_acc"], l + 1)
                V.tensor_copy(halves(glr[:, :]), PS[2][0:2 * RANK, :, 0:HALF]).then_inc(S["glr_done"], 1)
                V.memset(acc_a[:, :, :, :], 0.0)
                dve.wait_ge(S["zb_done"], l * 2 + 2)
                V.scalar_tensor_tensor(out=ex[:, 0:2, :], in0=bcum[:, :, :], scalar=-1.0, in1=bcum[:, :, :],
                                       op0=ALU.mult, op1=ALU.max).then_inc(S["abs_done"], 1)
                dve.wait_ge(S["ln_done"], l + 1)
                step("b_step", 2, V.scalar_tensor_tensor(out=bcum[:, :, :], in0=bcum[:, :, :], scalar=0.0,
                                                         in1=ex[:, 0:2, :], op0=ALU.min, op1=ALU.subtract))
                step("b_step", 2, V.tensor_tensor_scan(bcum[:, 0, :], chunk_mask[:, :], bcum[:, 0, :], 0.0,
                                                       ALU.mult, ALU.add))
                V.tensor_tensor_scan(bcum[:, 1, :], chunk_mask[:, :], bcum[:, 1, :], 0.0,
                                     ALU.mult, ALU.add).then_inc(S["b_done"], 1)
                dve.wait_ge(S["b_done"], l + 1)

                def chunks(ap, n=CH, upto=SEQ):
                    return ap[:, :, 0:upto].rearrange("p t (c i) -> p t c i", i=n)

                b4 = chunks(bcum)
                for t in range(2):
                    i = V.tensor_tensor(chunks(pair_exp[1])[:, t], b4[:, t, :, CH - 1:CH].to_broadcast([P, NCH, CH]),
                                        b4[:, t], ALU.subtract)
                i.then_inc(S["arg_done"], 1)
                dve.wait_ge(S["exp_done"], l * 9 + 1)
                V.tensor_copy(elast[:, :, :], chunks(pair_exp[0])[:, :, :, CH - 1])
                V.tensor_tensor(qe[:, :, :], qk[:, 0:2, :], pair_exp[0], ALU.mult).then_inc(S["qe_done"], 1)
                dve.wait_ge(S["qe_done"], l + 1)

                def arguments(i):
                    s = LEVELS[i]
                    upto = T if s <= META // 2 else SEQ
                    e = chunks(pair_exp[i % 2], 2 * s, upto)
                    b = chunks(bcum, 2 * s, upto)
                    nb = upto // (2 * s)
                    for t in range(2):
                        ref = b[:, t, :, s - 1:s].to_broadcast([P, nb, s])
                        V.tensor_tensor(e[:, t, :, 0:s], ref, b[:, t, :, 0:s], ALU.subtract)
                        x = V.tensor_tensor(e[:, t, :, s:2 * s], b[:, t, :, s:2 * s], ref, ALU.subtract)
                    x.then_inc(S["arg_done"], 1)

                def decayed(i):
                    s = LEVELS[i]
                    upto = T if s <= META // 2 else SEQ
                    dve.wait_ge(S["exp_done"], l * 9 + (i + 3))
                    if i >= 2:
                        dve.wait_ge(S["lev_acc"], l * 7 + (i - 1))
                    e = pair_exp[i % 2]
                    V.tensor_tensor(kt[:, i % 2, :, 0:upto], qk[:, 2:4, 0:upto], e[:, :, 0:upto],
                                    ALU.mult)
                    e = chunks(e, 2 * s, upto)
                    q = chunks(qk[:, 0:2, :], 2 * s, upto)
                    o = qt[:, i % 2, :, 0:upto // 2].rearrange("p t (c i) -> p t c i", i=s)
                    V.tensor_tensor(o, q[:, :, :, s:2 * s], e[:, :, :, s:2 * s], ALU.mult).then_inc(S["ktqt_done"], 1)
                    dve.wait_ge(S["ktqt_done"], l * 7 + (i + 1))

                def take_level(i):
                    s = LEVELS[i]
                    nb = CH // 2 // s
                    dve.wait_ge(S["masks"], 1)
                    dve.wait_ge(S["lev_acc"], l * 7 + (i + 1))
                    for hp in range(2):
                        dst = acc_a[:, 2 * hp:2 * hp + 2, :, :].rearrange("p h c (b i) -> p (h c) b i", i=2 * s)[:, :, :, s:2 * s]
                        src = PS[2][:, hp, :].rearrange("p (g b i) -> p g b i", b=nb, i=s)
                        msk = level_mask[:, i, :].rearrange("p (o b i) -> p o b i", o=1, i=s).to_broadcast([P, 8, nb, s])
                        x = V.copy_predicated(dst, msk, src)
                    if s <= META // 2:
                        nb = META // 2 // s
                        dst = acc_t[:, :, :].rearrange("p h (b i) -> p h b i", i=2 * s)[:, :, :, s:2 * s]
                        src = PS[3][0:META, 0, 0:32].rearrange("p (g b i) -> p g b i", b=nb, i=s)
                        msk = level_mask[0:META, i, 0:META // 2].rearrange("p (o b i) -> p o b i", o=1, i=s)\
                            .to_broadcast([META, HEADS, nb, s])
                        x = V.copy_predicated(dst, msk, src)
                    x.then_inc(S["lev_evac"], 1)
                    dve.wait_ge(S["lev_evac"], l * 7 + (i + 1))

                def v_tail_copy(h):
                    dve.wait_ge(S["vtr_acc"], l * 4 + (h + 1))
                    V.tensor_copy(v_tail[:, h, :], PS[3][0:META, 0, 256:256 + DV]).then_inc(S["v_tail_done"], 1)

                def pool_windows(g, idx):
                    u = ft[:, g % 2, :]
                    wait_stream(dve, l, idx)
                    if g < 2:
                        dve.wait_ge(S["vtr_acc"], l * 4 + (g + 3))
                    V.tensor_copy(halves(u), pair(idx % 2)).then_inc(S["u_evac"], 1)
                    dve.wait_ge(S["u_evac"], l * 4 + (g + 1))
                    src = u
                    for j in range(g + 1):
                        sh = 1 << j
                        dst = win[:, j % 2, :]
                        V.tensor_copy(dst[:, 0:sh], src[:, 0:sh])
                        step("pool_step", 14, V.tensor_tensor(dst[:, sh:T], src[:, sh:T], src[:, 0:T - sh], ALU.add))
                        src = dst
                    w = WINDOWS[g]
                    step("pool_step", 14, V.tensor_tensor(src[:, 0:w], src[:, 0:w], inv_count[:, 0:w], ALU.mult))
                    V.tensor_tensor(u[:, 0:w], src[:, 0:w], u[:, 0:w], ALU.subtract)
                    V.scalar_tensor_tensor(out=u[:, w:T], in0=src[:, w:T], scalar=1.0 / w, in1=u[:, w:T],
                                           op0=ALU.mult, op1=ALU.subtract).then_inc(S["pool_done"], 1)
                    dve.wait_ge(S["pool_done"], l * 4 + (g + 1))

                def pool_out(g, idx):
                    wait_stream(dve, l, idx)
                    ps_scale = par[:, C_PS + g:C_PS + g + 1]
                    V.tensor_scalar(halves(yp_hi[:, g, :]), pair(idx % 2), ps_scale, None, ALU.mult).then_inc(S["wsplit_step"], 1)
                    V.tensor_scalar(halves(win[:, 0, :]), pair(idx % 2), ps_scale, None, ALU.mult).then_inc(S["wsplit_step"], 1)
                    dve.wait_ge(S["wsplit_step"], l * 8 + (2 * g + 2))
                    V.tensor_tensor(yp_lo[:, g, :], win[:, 0, :], yp_hi[:, g, :].bitcast(F32),
                                    ALU.subtract).then_inc(S["w_evac"], 1)
                    dve.wait_ge(S["masks"], 1)
                    dve.wait_ge(S["w_evac"], l * 4 + (g + 1))

                def states(t):
                    dve.wait_ge(S["u_acc"], l * 2 + (t + 1))
                    step("s_step", 6, V.tensor_copy(state[:, t, 0, :], PS[3][:, 1, 0:DV]))
                    for c in range(1, NCH):
                        x = V.scalar_tensor_tensor(out=state[:, t, c, :], in0=state[:, t, c - 1, :],
                                                   scalar=elast[:, t, c:c + 1], in1=PS[3][:, 1, c * DV:(c + 1) * DV],
                                                   op0=ALU.mult, op1=ALU.add)
                        if c < NCH - 1:
                            step("s_step", 6, x)
                    x.then_inc(S["s_done"], 1)

                def take_o(h):
                    dve.wait_ge(S["o_acc"], l * 4 + (h + 1))
                    V.tensor_copy(qk[:, h, 0:SEQ], PS[2 + h % 2][:, 0, :])
                    V.tensor_copy(qk[:, h, TAIL:T], PS[2 + h % 2][:, 1, 0:META]).then_inc(S["o_done"], 1)

                def finish_o(h):
                    dve.wait_ge(S["rms_spread"], l * 4 + (h + 1))
                    V.tensor_tensor(halves(qk[:, h, :], span), halves(qk[:, h, :], span), pair(2 + h % 2, span),
                                    ALU.mult).then_inc(S["o_scaled"], 1)
                    dve.wait_ge(S["o_scaled"], l * 4 + (h + 1))
                    V.scalar_tensor_tensor(out=qk[:, h, tok], in0=qk[:, h, tok], scalar=par[:, C_GN + h:C_GN + h + 1],
                                           in1=s_r[:, h, tok], op0=ALU.mult, op1=ALU.mult).then_inc(S["o_fin"], 1)

                def split_o(h):
                    dve.wait_ge(S["o_hi_done"], l * 4 + (h + 1))
                    V.tensor_tensor(x_lo[:, h, tok], qk[:, h, tok], x_hi[:, h, tok].bitcast(F32),
                                    ALU.subtract).then_inc(S["o_lo_done"], 1)

                def take_pool_part(mo):
                    idx = 20 + mo
                    wait_stream(dve, l, idx)
                    V.scalar_tensor_tensor(out=halves(X[:, mo, :], span), in0=halves(X[:, mo, :], span), scalar=ALPHA,
                                           in1=pair(idx % 2, span), op0=ALU.mult, op1=ALU.add).then_inc(S["wop_evac"], 1)

                arguments(0)
                dve.wait_ge(S["exp_done"], l * 9 + 2)
                V.tensor_tensor(kdec[:, :, :], qk[:, 2:4, 0:SEQ], ex[:, 2:4, 0:SEQ], ALU.mult).then_inc(S["kdec_done"], 1)
                dve.wait_ge(S["kdec_done"], l + 1)
                arguments(1)
                decayed(0)
                dve.wait_ge(S["masks"], 1)
                dve.wait_ge(S["diag_acc"], l + 1)
                for hp in range(2):
                    V.copy_predicated(acc_a[:, 2 * hp:2 * hp + 2, :, :].rearrange("p h c i -> p (h c) i"),
                                      ident_mask[:, :].rearrange("p (o i) -> p o i", o=1).to_broadcast([P, 8, P]),
                                      PS[2 + hp][:, :, :].rearrange("p a (c i) -> p (a c) i", i=CH)).then_inc(S["diag_evac"], 1)
                arguments(2)
                decayed(1)
                arguments(3)
                dve.wait_ge(S["masks"], 1)
                dve.wait_ge(S["tdiag_acc"], l + 1)
                V.copy_predicated(acc_t[:, :, :], ident_mask[0:META, 0:META].rearrange("p (o i) -> p o i", o=1)
                                  .to_broadcast([META, HEADS, META]),
                                  PS[3][0:META, 0, 0:HEADS * META].rearrange("p (h i) -> p h i", i=META))
                v_tail_copy(0)
                take_level(0)
                decayed(2)
                arguments(4)
                v_tail_copy(1)
                take_level(1)
                decayed(3)
                arguments(5)
                v_tail_copy(2)
                take_level(2)
                pool_windows(0, 8)
                v_tail_copy(3)
                decayed(4)
                arguments(6)
                pool_windows(1, 9)
                pool_out(0, 10)
                take_level(3)
                decayed(5)
                pool_windows(2, 11)
                pool_out(1, 12)
                take_level(4)
                decayed(6)
                pool_windows(3, 13)
                pool_out(2, 14)
                take_level(5)
                pool_out(3, 16)
                take_level(6)
                states(0)
                states(1)
                for h in range(HEADS):
                    take_o(h)
                for mo in range(2):
                    take_pool_part(mo)
                dve.wait_ge(S["rms_std"], l + 1)
                n_quarter = (T - span[0]) // QUARTERS
                V.reciprocal(rms_rows[:, 0:n_quarter], rms_rows[:, 0:n_quarter]).then_inc(S["rms_inv"], 1)
                take_pool_part(2)
                take_pool_part(3)
                finish_o(0)
                finish_o(1)
                take_pool_part(4)
                split_o(0)
                take_pool_part(5)
                split_o(1)
                finish_o(2)
                finish_o(3)
                take_pool_part(6)
                split_o(2)
                split_o(3)
                take_pool_part(7)
                dve.wait_ge(S["wop_evac"], l * 8 + 8)
                resid(l * LN_PER + 1, lambda mo: stream_ready(l, 28 + mo), 2, span)

            for ap, val in ((ones_mean[:, :], 1.0 / D), (ones[:, :], 1.0), (rms_comb[:, :], 0.0), (chunk_mask[:, :], 1.0),
                            (warm[:, :], 1.0), (rms_eps[:, :], RMS_EPS)):
                i = V.memset(ap, val)
            i.then_inc(S["setup"], 1)
            dve.wait_ge(S["setup"], 1)
            for t in range(META):
                V.memset(inv_count[:, t:t + 1], 1.0 / (t + 1))
            V.memset(rms_comb[:, RMS_ROWS - 1:RMS_ROWS], 1.0 / DV)
            for c in range(1, NCH + 1):
                V.memset(chunk_mask[:, c * CH:c * CH + 1], 0.0)
            V.memset(chunk_mask[:, 0:1], 0.0).then_inc(S["consts_dve"], 1)
            for kind, n in START_LOW_ORDER:
                if kind == "piece":
                    dve.wait_ge(S["raw_hi"], n + 1)
                    V.tensor_tensor(w_lo[:, n, :], raw_first[:, n, :], w_hi[:, n, :].bitcast(F32),
                                    ALU.subtract).then_inc(S["split_done"], 1)
                else:
                    if n == 0:
                        dve.wait_ge(S["x_hi_first"], 1)
                    dve.wait_ge(S["x_hi_done"], n + 1)
                    V.tensor_tensor(x_lo[:, n, :], X[:, n, :], x_hi[:, n, :].bitcast(F32),
                                    ALU.subtract).then_inc(S["x_lo_done"], 1)
            dve.wait_ge(S["consts_dve"], 1)

            def layer(l, span):
                ffn(l, 0, ALL)
                norm(l * LN_PER, ALL)
                mixer(l, span)
                norm(l * LN_PER + 1, span)
                ffn(l, 1, span)
                norm(l * LN_PER + 2, span, final=span == OWN)

            with dve.Fori(0, DEPTH - 1) as l:
                layer(l, ALL)
            layer(DEPTH - 1, OWN)


def place(h):
    return 2 * (h % 2) + h // 2


def tiles(w):
    k, m = w.shape
    return w.reshape(k // 128, 128, m // 128, 128).transpose(2, 1, 0, 3)


def kernel(x, meta_tokens, ffn1_w_gate, ffn1_w_up, ffn1_w_down, ln1_g, ln1_b, w_in, w_gate_up, b_gate, w_pool,
           pool_scale, gla_norm_g, w_out, ln2_g, ln2_b, ffn2_w_gate, ffn2_w_up, ffn2_w_down, ln3_g, ln3_b):
    import numpy as np
    import concourse.bacc as bacc
    from concourse.bass_utils import run_bass_kernel_spmd

    A = np.asarray
    x_t = np.ascontiguousarray(np.concatenate([A(meta_tokens), A(x)[0]], axis=0).T)
    stream = np.zeros((DEPTH * LAYER_PIECES, P, TILES, P), A(w_in).dtype)
    params = np.zeros((DEPTH, P, C_ALL), A(w_in).dtype)

    n = 0
    for l in range(DEPTH):
        for f, (wg, wu, wd) in enumerate(((ffn1_w_gate, ffn1_w_up, ffn1_w_down), (ffn2_w_gate, ffn2_w_up, ffn2_w_down))):
            g, u, d = (tiles(A(w)[l]) for w in (wg, wu, wd))
            for m0, nm in PHASES:
                for m in range(m0, m0 + nm):
                    stream[n] = g[m]
                    stream[n + 1] = u[m]
                    n += 2
                stream[n:n + KC, :, 0:nm] = d[:, :, m0:m0 + nm]
                n += KC
            if f == 0:
                stream[n:n + MIX_IN] = tiles(A(w_in)[l][:, :16 * P])[list(IN_TILES)]
                n += MIX_IN
                wo = tiles(A(w_out)[l])
                for part in range(2):
                    for mo in range(0, KC, 2):
                        stream[n, :, 0:4] = wo[mo, :, 4 * part:4 * part + 4]
                        stream[n, :, 4:8] = wo[mo + 1, :, 4 * part:4 * part + 4]
                        n += 1
        for r, (g, b) in enumerate(((ln1_g, ln1_b), (ln2_g, ln2_b), (ln3_g, ln3_b))):
            params[l, :, C_LN + 16 * r:C_LN + 16 * r + 8] = A(g)[l].reshape(KC, P).T
            params[l, :, C_LN + 16 * r + 8:C_LN + 16 * r + 16] = A(b)[l].reshape(KC, P).T
        params[l, :, C_BG:C_BG + 2] = A(b_gate)[l].reshape(2, P).T
        params[l, :, C_PS:C_PS + 4] = A(pool_scale)[l].reshape(4, P).T
        params[l, :, C_GN:C_GN + 4] = A(gla_norm_g)[l].reshape(4, P).T
        params[l, :, C_WP:C_GU] = A(w_pool)[l].transpose(1, 0, 2).reshape(P, GROUPS * P)
        params[l, 0:RANK, C_GU:C_GL] = params[l, RANK:2 * RANK, C_GU:C_GL] = A(w_gate_up)[l]
        params[l, :, C_GL:C_ALL] = A(w_in)[l][:, 16 * P:].reshape(KC, P, RANK).transpose(1, 0, 2).reshape(P, KC * RANK)
    stream = stream.reshape(DEPTH * LAYER_PIECES // RAWS, RAWS, P, PIECE)

    nc = bacc.Bacc("TRN2", target_bir_lowering=False, num_devices=1)
    arrays = {"in_x_t": x_t, "in_stream": stream, "in_params": params}
    aps = [nc.dram_tensor(name, a.shape, F32, kind="ExternalInput").ap() for name, a in arrays.items()]
    out = nc.dram_tensor("out_t", (D, SEQ), F32, kind="ExternalOutput").ap()
    build(nc, *aps, out)
    r = run_bass_kernel_spmd(nc, [arrays], core_ids=[0])
    return np.ascontiguousarray(r.results[0]["out_t"].T)[None]
```
